# Optimizing a Trainium2 kernel written in Bass

```python
import jax, jax.numpy as jnp
from jax import lax
import numpy as np

D_MODEL = 1024
BATCH = 1
SEQ = 1024
DEPTH = 2

CHUNK = 64
N_A_LAYERS = DEPTH // 2
N_B_LAYERS = DEPTH - N_A_LAYERS
GMLP_BLOCK = 128
GMLP_FFN = 4 * D_MODEL
GMLP_HALF = GMLP_FFN // 2
GMLP_GROUPS = 8
GMLP_GROUP_DIM = GMLP_HALF // GMLP_GROUPS
HEAD_DIM = 64
N_Q_HEADS = D_MODEL // HEAD_DIM
N_KV_HEADS = max(N_Q_HEADS // 8, 1)
Q_PER_KV = N_Q_HEADS // N_KV_HEADS
WINDOW = 128
WINDOW_CHUNKS = WINDOW // CHUNK
ROPE_THETA = 10000.0
D_FF = -(-8 * D_MODEL // (3 * 256)) * 256
EPS = 1e-6
MASK_VALUE = -1e30

kernel_name = "yoco_gmlp_swa_sink_hybrid"

def rms_norm(x, g):
    xf = x.astype(jnp.float32)
    y = xf * lax.rsqrt(jnp.mean(xf * xf, axis=-1, keepdims=True) + EPS)
    return (y * g.astype(jnp.float32)).astype(x.dtype)

def layer_norm(x, g, b):
    xf = x.astype(jnp.float32)
    mu = jnp.mean(xf, axis=-1, keepdims=True)
    var = jnp.mean(jnp.square(xf - mu), axis=-1, keepdims=True)
    y = (xf - mu) * lax.rsqrt(var + EPS)
    return (y * g.astype(jnp.float32) + b.astype(jnp.float32)).astype(x.dtype)

def rope_tables(seq):
    pos = jnp.arange(seq, dtype=jnp.float32)
    inv = 1.0 / (jnp.float32(ROPE_THETA) ** (jnp.arange(0, HEAD_DIM, 2, dtype=jnp.float32) / HEAD_DIM))
    ang = pos[:, None] * inv[None, :]
    return jnp.cos(ang), jnp.sin(ang)

def apply_rope(t, cos, sin):
    tf = t.astype(jnp.float32)
    t1, t2 = jnp.split(tf, 2, axis=-1)
    c = cos[None, :, None, :]
    s = sin[None, :, None, :]
    out = jnp.concatenate([t1 * c - t2 * s, t2 * c + t1 * s], axis=-1)
    return out.astype(t.dtype)

def gmlp_block_mask():
    i = jnp.arange(GMLP_BLOCK)
    return (i[None, :] // CHUNK) <= (i[:, None] // CHUNK)

def gmlp_mixer(hn, w_in, b_in, ln_g, ln_b, w_s, b_s, w_out):
    bsz, seq, _ = hn.shape
    z = jax.nn.gelu(hn @ w_in + b_in)
    u, v = jnp.split(z, 2, axis=-1)
    v = layer_norm(v, ln_g, ln_b)
    nb = seq // GMLP_BLOCK
    v = v.reshape(bsz, nb, GMLP_BLOCK, GMLP_GROUPS, GMLP_GROUP_DIM)
    ws = jnp.where(gmlp_block_mask()[None], w_s, jnp.zeros_like(w_s))
    mixed = jnp.einsum('gij,bnjgd->bnigd', ws, v) + b_s.T[None, None, :, :, None]
    gated = u * mixed.reshape(bsz, seq, GMLP_HALF)
    return gated @ w_out

def shift_chunks(t, s):
    if s == 0:
        return t
    return jnp.concatenate([jnp.zeros_like(t[:, :s]), t[:, :-s]], axis=1)

def shared_kv(h, kv_norm, w_kv, cos, sin):
    bsz, seq, _ = h.shape
    nc = seq // CHUNK
    kv = rms_norm(h, kv_norm) @ w_kv
    k, v = jnp.split(kv, 2, axis=-1)
    k = apply_rope(k.reshape(bsz, seq, N_KV_HEADS, HEAD_DIM), cos, sin)
    v = v.reshape(bsz, seq, N_KV_HEADS, HEAD_DIM)
    k = k.reshape(bsz, nc, CHUNK, N_KV_HEADS, HEAD_DIM)
    v = v.reshape(bsz, nc, CHUNK, N_KV_HEADS, HEAD_DIM)
    shifts = list(range(WINDOW_CHUNKS - 1, -1, -1))
    k_band = jnp.concatenate([shift_chunks(k, s) for s in shifts], axis=2)
    v_band = jnp.concatenate([shift_chunks(v, s) for s in shifts], axis=2)
    return k_band, v_band

def band_valid(nc):
    m = jnp.arange(WINDOW_CHUNKS * CHUNK)
    shift_of_m = (WINDOW_CHUNKS - 1) - m // CHUNK
    n = jnp.arange(nc)
    return (n[:, None] - shift_of_m[None, :]) >= 0

def swa_sink_mixer(hn, k_band, v_band, w_q, sinks, w_o, cos, sin):
    bsz, seq, _ = hn.shape
    nc = seq // CHUNK
    q = apply_rope((hn @ w_q).reshape(bsz, seq, N_Q_HEADS, HEAD_DIM), cos, sin)
    q = q.reshape(bsz, nc, CHUNK, N_KV_HEADS, Q_PER_KV, HEAD_DIM)
    scale = 1.0 / np.sqrt(HEAD_DIM)
    s = jnp.einsum('bnckgd,bnmkd->bnkgcm', q, k_band,
                   preferred_element_type=jnp.float32) * scale
    valid = band_valid(nc)[None, :, None, None, None, :]
    s = jnp.where(valid, s, MASK_VALUE)
    sink = sinks.astype(jnp.float32).reshape(N_KV_HEADS, Q_PER_KV)[None, None, :, :, None, None]
    mx = jnp.maximum(jnp.max(s, axis=-1, keepdims=True), sink)
    p = jnp.exp(s - mx)
    p = p / (jnp.sum(p, axis=-1, keepdims=True) + jnp.exp(sink - mx))
    o = jnp.einsum('bnkgcm,bnmkd->bnckgd', p.astype(v_band.dtype), v_band)
    return o.reshape(bsz, seq, N_Q_HEADS * HEAD_DIM) @ w_o

def swiglu(hn, w_gate_up, w_down):
    gate, up = jnp.split(hn @ w_gate_up, 2, axis=-1)
    return (jax.nn.silu(gate) * up) @ w_down

def setup_inputs(seed: int = 0) -> dict:
    key = jax.random.key(seed)
    ks = jax.random.split(key, 24)
    f32 = jnp.float32
    nrm = lambda k, shape, sc: jax.random.normal(k, shape, f32) * sc
    gain = lambda k, shape: 1.0 + 0.02 * jax.random.normal(k, shape, f32)
    return {
        "x": jax.random.normal(ks[0], (BATCH, SEQ, D_MODEL), f32),
        "norm_mix_pre": gain(ks[1], (DEPTH, D_MODEL)),
        "norm_mix_post": gain(ks[2], (DEPTH, D_MODEL)),
        "norm_ffn_pre": gain(ks[3], (DEPTH, D_MODEL)),
        "norm_ffn_post": gain(ks[4], (DEPTH, D_MODEL)),
        "a_w_in": nrm(ks[5], (N_A_LAYERS, D_MODEL, GMLP_FFN), D_MODEL ** -0.5),
        "a_b_in": nrm(ks[6], (N_A_LAYERS, GMLP_FFN), 0.02),
        "a_ln_g": gain(ks[7], (N_A_LAYERS, GMLP_HALF)),
        "a_ln_b": nrm(ks[8], (N_A_LAYERS, GMLP_HALF), 0.02),
        "a_w_s": nrm(ks[9], (N_A_LAYERS, GMLP_GROUPS, GMLP_BLOCK, GMLP_BLOCK), GMLP_BLOCK ** -0.5),
        "a_b_s": gain(ks[10], (N_A_LAYERS, GMLP_GROUPS, GMLP_BLOCK)),
        "a_w_out": nrm(ks[11], (N_A_LAYERS, GMLP_HALF, D_MODEL), GMLP_HALF ** -0.5),
        "kv_norm": gain(ks[12], (D_MODEL,)),
        "w_kv": nrm(ks[13], (D_MODEL, 2 * N_KV_HEADS * HEAD_DIM), D_MODEL ** -0.5),
        "b_w_q": nrm(ks[14], (N_B_LAYERS, D_MODEL, N_Q_HEADS * HEAD_DIM), D_MODEL ** -0.5),
        "b_sinks": nrm(ks[15], (N_B_LAYERS, N_Q_HEADS), 1.0),
        "b_w_o": nrm(ks[16], (N_B_LAYERS, N_Q_HEADS * HEAD_DIM, D_MODEL), (N_Q_HEADS * HEAD_DIM) ** -0.5),
        "f_w_gate_up": nrm(ks[17], (DEPTH, D_MODEL, 2 * D_FF), D_MODEL ** -0.5),
        "f_w_down": nrm(ks[18], (DEPTH, D_FF, D_MODEL), D_FF ** -0.5),
    }

def reference(x, norm_mix_pre, norm_mix_post, norm_ffn_pre, norm_ffn_post,
              a_w_in, a_b_in, a_ln_g, a_ln_b, a_w_s, a_b_s, a_w_out,
              kv_norm, w_kv, b_w_q, b_sinks, b_w_o, f_w_gate_up, f_w_down):
    seq = x.shape[1]
    cos, sin = rope_tables(seq)
    h = x
    k_band = None
    v_band = None
    for layer in range(DEPTH):
        if layer == N_A_LAYERS:
            k_band, v_band = shared_kv(h, kv_norm, w_kv, cos, sin)
        hn = rms_norm(h, norm_mix_pre[layer])
        if layer < N_A_LAYERS:
            a = layer
            mix = gmlp_mixer(hn, a_w_in[a], a_b_in[a], a_ln_g[a], a_ln_b[a],
                             a_w_s[a], a_b_s[a], a_w_out[a])
        else:
            b = layer - N_A_LAYERS
            mix = swa_sink_mixer(hn, k_band, v_band, b_w_q[b], b_sinks[b], b_w_o[b], cos, sin)
        h = h + rms_norm(mix, norm_mix_post[layer])
        ff = swiglu(rms_norm(h, norm_ffn_pre[layer]), f_w_gate_up[layer], f_w_down[layer])
        h = h + rms_norm(ff, norm_ffn_post[layer])
    return h


_drawn_inputs = setup_inputs


def setup_inputs(seed=0):
    import zlib

    import numpy as np

    out = dict(_drawn_inputs(seed))
    spreads = {}
    factors = {'norm_ffn_post': 3.617,
     'a_ln_g': 13.704,
     'a_ln_b': 13.962,
     'a_b_s': 12.205,
     'kv_norm': 18.281,
     'b_sinks': 64.0}
    for name, (base, spread) in spreads.items():
        noise = np.random.default_rng([zlib.crc32(name.encode()), seed]).standard_normal(out[name].shape)
        drawn = base * np.exp(spread * noise) if base else spread * noise
        out[name] = __import__('jax').numpy.asarray(drawn.astype(out[name].dtype))
    for name, factor in factors.items():
        out[name] = (out[name] * factor).astype(out[name].dtype)
    return out
```

```python
import numpy as np

import concourse.bass as bass
from concourse import mybir
from concourse.alu_op_type import AluOpType as ALU

F32 = mybir.dt.float32
F32R = mybir.dt.float32r
ACT = mybir.ActivationFunctionType
AX_X = mybir.AxisListType.X
ds = bass.ds

P = 128
D = 1024
S = 1024
KT = D // P
TT = S // P
HALF = 512
GMLP_FFN = 4 * D
GMLP_HALF = GMLP_FFN // 2
GROUPS = 8
PAIR = 2 * P
assert GMLP_HALF // GROUPS == PAIR
D_FF = -(-8 * D // (3 * 256)) * 256
HEAD = 64
CHUNK = 64
NCHUNK = S // CHUNK
SCALE = 1.0 / float(np.sqrt(HEAD))
EPS = 1e-6
GMLP_CHUNKS = GMLP_HALF // PAIR
FFN_CHUNKS = D_FF // PAIR
V_TILES = GMLP_HALF // P
Q_PAIRS = D // PAIR
G, U, W2 = 0, 1, 2

GAIN_MIX = (0, 8)
GAIN_FFN = (16, 24)
GAIN_KV = 32
BIAS_IN = 40
NCOLS = BIAS_IN + GMLP_FFN // P

STAGE_GMLP = 0
STAGE_FFN = (2 * GMLP_CHUNKS, 2 * GMLP_CHUNKS + 2 * FFN_CHUNKS)
STAGES = STAGE_FFN[1] + 2 * FFN_CHUNKS
DOWN_GMLP = 0
DOWN_FFN0 = 2 * GMLP_CHUNKS
DOWN_O = DOWN_FFN0 + 2 * FFN_CHUNKS
DOWN_FFN1 = DOWN_O + 2 * Q_PAIRS
DOWN_END = DOWN_FFN1 + 2 * FFN_CHUNKS
DOWN_BANKS = 8
USE_V = (0, None, 0)
USE_GMLP = (V_TILES // 4, 0, V_TILES // 4)
USE_FFN0 = (USE_GMLP[0] + GMLP_CHUNKS, GMLP_CHUNKS, USE_GMLP[2] + GMLP_CHUNKS)
USE_KV = tuple(u + FFN_CHUNKS for u in USE_FFN0)
USE_Q = (USE_KV[0] + 1, USE_KV[1], USE_KV[2])
USE_O = (USE_Q[0] + Q_PAIRS // 2, USE_Q[1] + Q_PAIRS // 2, USE_Q[2])
USE_FFN1 = (USE_O[0], USE_O[1], USE_O[2] + Q_PAIRS)
PROJ_V = 0
PROJ_KV = PROJ_V + 2 * V_TILES
PROJ_Q = PROJ_KV + 4
PROJ_END = PROJ_Q + 2 * (D // P)
TR_COLS = 1
TR_NORM = lambda n: TR_COLS + 2 * TT * n + (2 if n else 0)
TR_WS = TR_COLS + 2 * TT
NKV = 2
NPAIR = 4


def wait_apart(eng, sem, value):
    eng.wait_ge(sem, value)
    eng.nop(nofuse=True)


def build_trunk(nc, x, norm_mix_pre, norm_mix_post, norm_ffn_pre, norm_ffn_post, a_w_in, a_b_in, a_ln_g,
                a_ln_b, a_w_s, a_b_s, a_w_out, kv_norm, w_kv, b_w_q, b_sinks, b_w_o, f_w_gate_up,
                f_w_down, rope_cos, rope_sin, out):
    KB = 1024
    place = {"at": -(-nc.sbuf_base // 64) * 64}

    def sb(name, shape, dtype=F32, at=None):
        size = int(np.prod(shape[1:])) * 4
        if at is None:
            at = place["at"]
            place["at"] = -(-(at + size) // 64) * 64
        t = nc.alloc_sbuf_tensor_at(name, list(shape), dtype, offset=at)
        return t

    here = lambda: place["at"]

    acc = sb("acc", [P, TT, D])
    XH = sb("XH", [P, KT, S], F32R)
    XL = sb("XL", [P, KT, S], F32R)
    WH = [sb(f"WH{s}", [P, 8 * PAIR], F32R) for s in range(3)]
    WL = [sb(f"WL{s}", [P, 8 * PAIR], F32R) for s in range(3)]
    raw = [sb(f"raw{s}", [P, 8 * PAIR]) for s in range(3)]
    at_hid = here()
    hidH = sb("hidH", [P, 2, HALF], F32R)
    hidL = sb("hidL", [P, 2, HALF], F32R)
    junk = sb("junk", [P, 2, D], at=at_hid)
    vshift = sb("vshift", [P, TT, P], at=at_hid)
    at_sg = here()
    sg = sb("sg", [P, 2, HALF])
    rt = sb("rt", [P, D], at=at_sg)
    gpost = sb("gpost", [P, D])
    at_e = here()
    hin = sb("hin", [P, 2, D])
    hout = sb("hout", [P, 2, D])
    wsH = sb("wsH", [P, GROUPS, P], F32R, at=at_e)
    wsL = sb("wsL", [P, GROUPS, P], F32R, at=at_e + 4 * KB)
    bs = sb("bs", [P, GROUPS, P], at=at_e + 8 * KB)
    lngb = sb("lngb", [P, 2, PAIR], at=at_e + 12 * KB)
    stats = sb("stats", [P, TT, V_TILES, 6], at=at_e + 14 * KB)
    place["at"] = at_e + 17 * KB
    kT = sb("kT", [P, S], at=at_e)
    vt = sb("vt", [P, TT, P], at=at_e + 4 * KB)
    cosT = sb("cosT", [P, S], at=at_e + 8 * KB)
    sinT = sb("sinT", [P, S], at=at_e + 12 * KB)
    ident = sb("ident", [P, P])
    cols = sb("cols", [P, NCOLS])
    sink = sb("sink", [P, NKV, NPAIR])
    vmean = sb("vmean", [P, TT, 2])
    vrstd = sb("vrstd", [P, TT])
    ssq = sb("ssq", [P, 2])
    rms = sb("rms", [P, 2])
    root = sb("root", [P, 2])
    rstd = sb("rstd", [P, 2])
    a_max = sb("a_max", [P, NKV, NPAIR])
    a_neg = sb("a_neg", [P, NKV, NPAIR])
    a_off = sb("a_off", [P, NKV, NPAIR])
    a_snk = sb("a_snk", [P, NKV, NPAIR])
    a_sum = sb("a_sum", [P, NKV, NPAIR])
    a_den = sb("a_den", [P, NKV, NPAIR])
    a_inv = sb("a_inv", [P, NKV, NPAIR])
    qcH = [WH[1][:, e * 1024:e * 1024 + 512].rearrange("p (t c) -> p t c", t=KT) for e in range(2)]
    qcL = [WL[1][:, e * 1024:e * 1024 + 512].rearrange("p (t c) -> p t c", t=KT) for e in range(2)]
    kcH = [WH[1][:, e * 1024 + 512:e * 1024 + 640] for e in range(2)]
    kcL = [WL[1][:, e * 1024 + 512:e * 1024 + 640] for e in range(2)]
    vcH = [WH[1][:, e * 1024 + 640:e * 1024 + 768] for e in range(2)]
    vcL = [WL[1][:, e * 1024 + 640:e * 1024 + 768] for e in range(2)]
    pTH = [WH[0][:, k * HALF:(k + 1) * HALF] for k in range(NKV)]
    pTL = [WL[0][:, k * HALF:(k + 1) * HALF] for k in range(NKV)]
    prob = [raw[0][:, k * HALF:(k + 1) * HALF].rearrange("p (j m) -> p j m", j=NPAIR) for k in range(NKV)]
    qplain = [raw[2][:, e * 1024:e * 1024 + 512] for e in range(2)]
    qrot = [raw[2][:, e * 1024 + 512:(e + 1) * 1024] for e in range(2)]
    qT = acc

    bank = [nc.alloc_psum_tensor(f"bank{b}", [P, HALF], F32) for b in range(8)]

    h_dram = [nc.dram_tensor(f"h{n}", [TT, P, D], F32, kind="Internal").ap() for n in range(1, 4)]
    v_dram = nc.dram_tensor("v_park", [GMLP_CHUNKS, P, TT * PAIR], F32, kind="Internal").ap()
    x_in = x.rearrange("a (m p) d -> (a m) p d", p=P)
    out_t = out.rearrange("a (m p) d -> (a m) p d", p=P)
    h_from = [x_in, x_in, h_dram[0], h_dram[1], h_dram[2]]
    h_to = [None, h_dram[0], h_dram[1], h_dram[2], out_t]
    post_gain = [None, norm_mix_post[0:1, :], norm_ffn_post[0:1, :], norm_mix_post[1:2, :], norm_ffn_post[1:2, :]]

    sem = nc.alloc_semaphore
    loaded = [sem(f"loaded{s}") for s in range(3)]
    normed_v = sem("normed_v")
    w_ready = [sem(f"w_ready{s}") for s in range(3)]
    pool_step = sem("pool_step")
    proj_full = sem("proj_full")
    act_full = sem("act_full")
    act_ready = sem("act_ready")
    mul_full = sem("mul_full")
    prod_ready = sem("prod_ready")
    hid_hi = sem("hid_hi")
    hid_lo = sem("hid_lo")
    down_full = sem("down_full")
    down_added = sem("down_added")
    acc_zero = sem("acc_zero")
    tr_full = sem("tr_full")
    tr_hi = sem("tr_hi")
    tr_free = sem("tr_free")
    h_loaded = [sem(f"h_loaded{e}") for e in range(2)]
    h_stored = [sem(f"h_stored{e}") for e in range(2)]
    h_new = sem("h_new")
    g_loaded = sem("g_loaded")
    sq_done = sem("sq_done")
    ms_done = sem("ms_done")
    root_done = sem("root_done")
    rstd_done = sem("rstd_done")
    scaled = sem("scaled")
    rt_ready = sem("rt_ready")
    consts = sem("consts")
    ws_loaded = sem("ws_loaded")
    rope_loaded = sem("rope_loaded")
    ident_done = sem("ident_done")
    ws_masked = sem("ws_masked")
    sink_loaded = sem("sink_loaded")
    bs_loaded = sem("bs_loaded")
    gain_step = sem("gain_step")
    split_step = sem("split_step")
    prep_hi = sem("prep_hi")
    v_act = sem("v_act")
    vtr_full = sem("vtr_full")
    vtr_free = sem("vtr_free")
    v_parked = sem("v_parked")
    v_stat = sem("v_stat")
    v_root = sem("v_root")
    ln_step = sem("ln_step")
    bias_done = sem("bias_done")
    q_copied = sem("q_copied")
    rope_step = sem("rope_step")
    q_done = sem("q_done")
    v_copied = sem("v_copied")
    prep = sem("prep")
    s_full = sem("s_full")
    s_max = sem("s_max")
    s_exp = sem("s_exp")
    s_norm = sem("s_norm")
    p_full = sem("p_full")
    p_hi = sem("p_hi")
    p_lo = sem("p_lo")
    o_full = sem("o_full")
    o_hi = sem("o_hi")
    o_lo = sem("o_lo")

    def f(ap):
        return ap.bitcast(F32)

    def in_tile(t, b):
        v = t[:, :].rearrange("p (k f) -> p k f", k=KT)
        return lambda k: v[:, k, b * P:(b + 1) * P]

    with nc.Block() as block:
        @block.sync
        def _(sp):
            def load_in(s, use, src, first=False):
                if not first:
                    sp.wait_ge(w_ready[s], use)
                sp.dma_start(raw[s][:, :].rearrange("p (k f) -> p k f", k=KT),
                             src.rearrange("(k p) f -> p k f", p=P)).then_inc(loaded[s], 16)

            def load_down(use, src, first=False):
                if not first:
                    sp.wait_ge(w_ready[W2], use)
                sp.dma_start(raw[W2][:, :].rearrange("p (t n) -> p t n", t=2),
                             src.rearrange("(t p) n -> p t n", p=P)).then_inc(loaded[W2], 16)

            def norm_loads(n):
                if n:
                    sp.dma_start(gpost[:, :], post_gain[n].to_broadcast([P, D])).then_inc(g_loaded, 16)
                for m in range(2):
                    sp.dma_start(hin[:, m, :], h_from[n][m]).then_inc(h_loaded[m], 16)

            def norm_tile(n, m, par, more):
                if n:
                    sp.wait_ge(h_new, TT * (n - 1) + m + 1)
                    sp.dma_start(h_to[n][ds(m, 1)].rearrange("a p d -> (a p) d"), hout[:, par, :]).then_inc(h_stored[par], 16)
                else:
                    sp.wait_ge(rt_ready, m + 1)
                if more:
                    sp.dma_start(hin[:, par, :], h_from[n][ds(m + 2, 1)].rearrange("a p d -> (a p) d")).then_inc(h_loaded[par], 16)

            def norm(n):
                with sp.Fori(0, TT // 2 - 1) as j:
                    for par in range(2):
                        norm_tile(n, j * 2 + par, par, True)
                for m in (TT - 2, TT - 1):
                    norm_tile(n, m, m % 2, False)

            def ffn(layer):
                use = (USE_FFN0, USE_FFN1)[layer]
                gu, down = f_w_gate_up[layer], f_w_down[layer]

                def chunk(c):
                    load_in(G, use[G] + c, gu[:, ds(c * PAIR, PAIR)])
                    load_in(U, use[U] + c, gu[:, ds(c * PAIR + D_FF, PAIR)])
                    load_down(use[W2] + c, down[ds(c * PAIR, PAIR), :])
                return chunk

            rows = sg[:, 0, 0:P]
            srcs = [norm_mix_pre[0], norm_mix_pre[1], norm_ffn_pre[0], norm_ffn_pre[1], kv_norm, a_b_in[0]]
            at = 0
            for src in srcs:
                r = src.rearrange("(k p) -> k p", p=P)
                sp.dma_start(rows[at:at + r.shape[0], :], r).then_inc(consts, 16)
                at += r.shape[0]
            norm_loads(0)
            w_in = a_w_in[0]
            load_in(G, 0, w_in[:, GMLP_HALF:GMLP_HALF + PAIR], first=True)
            load_in(W2, 0, w_in[:, GMLP_HALF + PAIR:GMLP_HALF + 2 * PAIR], first=True)
            sp.dma_start(gpost[:, :].rearrange("p (g j) -> p g j", g=GROUPS),
                         a_w_s[0].rearrange("g i j -> i g j")).then_inc(ws_loaded, 16)
            for g in range(NKV):
                for t in range(2):
                    sp.dma_start(sink[t * HEAD:(t + 1) * HEAD, g, :],
                                 b_sinks[0:1, g * 8 + t:(g + 1) * 8:2].to_broadcast([HEAD, NPAIR]),
                                 allow_slow_non_contiguous=True).then_inc(sink_loaded, 16)
            norm(0)
            sp.wait_ge(rt_ready, TT)
            sp.dma_start(bs[:, :, :].rearrange("p g i -> p (g i)"),
                         a_b_s[0:1].rearrange("a g i -> a (g i)").to_broadcast([P, D])).then_inc(bs_loaded, 16)

            def park_v(g):
                sp.wait_ge(vtr_free, g * 4 + 4)
                sp.dma_start(v_dram[ds(g, 1)].rearrange("a p n -> (a p) n"), raw[U][:, :]).then_inc(v_parked, 16)

            with sp.Fori(0, V_TILES // 4 - 1) as i:
                for e, s in enumerate((G, W2)):
                    load_in(s, i + 1, w_in[:, ds((i * 2 + 2 + e) * PAIR + GMLP_HALF, PAIR)])
                    park_v(i * 2 + e)
            last = V_TILES // 4 - 1
            load_in(G, USE_GMLP[G], w_in[:, 0:PAIR])
            park_v(2 * last)
            load_down(USE_GMLP[W2], a_w_out[0, 0:PAIR, :])
            park_v(2 * last + 1)

            def load_v(g):
                sp.dma_start(raw[U][:, :], v_dram[ds(g, 1)].rearrange("a p n -> (a p) n")).then_inc(loaded[U], 16)
                for e, src in enumerate((a_ln_g, a_ln_b)):
                    sp.dma_start(lngb[:, e, :], src[0:1, ds(g * PAIR, PAIR)].to_broadcast([P, PAIR])).then_inc(loaded[U], 16)

            sp.wait_ge(v_parked, 16 * GMLP_CHUNKS)
            load_v(0)
            with sp.Fori(1, GMLP_CHUNKS) as g:
                load_in(G, g + USE_GMLP[G], w_in[:, ds(g * PAIR, PAIR)])
                sp.wait_ge(w_ready[U], g)
                load_v(g)
                load_down(g + USE_GMLP[W2], a_w_out[0, ds(g * PAIR, PAIR), :])

            chunk = ffn(0)
            chunk(0)
            sp.wait_ge(prod_ready, 2 * 2 * GMLP_CHUNKS)
            norm_loads(1)
            norm(1)
            with sp.Fori(1, FFN_CHUNKS) as c:
                chunk(c)

            load_in(G, USE_KV[G], w_kv)
            for par in range(2):
                sp.wait_ge(h_stored[par], 16 * (TT // 2))
            norm_loads(2)
            norm(2)
            for par in range(2):
                sp.wait_ge(h_stored[par], 16 * (TT // 2) * 2)
            sp.wait_ge(rt_ready, TT * 3)
            sp.dma_start(cosT[:, :], rope_cos).then_inc(rope_loaded, 16)
            sp.dma_start(sinT[:, :], rope_sin).then_inc(rope_loaded, 16)

            def load_q(s, use, j):
                sp.wait_ge(w_ready[s], use)
                for b in range(2):
                    for g in range(NKV):
                        dst = raw[s][:, :].rearrange("p (k b g f) -> p k b g f", k=KT, b=2, g=NKV)[:, :, b, g, :]
                        at = (g * 8 + j * 2 + b) * HEAD
                        src = b_w_q[0][:, at:at + HEAD].rearrange("(k p) f -> p k f", p=P)
                        sp.dma_start(dst, src).then_inc(loaded[s], 16)

            for j in range(Q_PAIRS):
                load_q((U, G)[j % 2], (USE_Q[U], USE_Q[G])[j % 2] + j // 2, j)

            def load_o(j):
                if j:
                    sp.wait_ge(w_ready[W2], USE_O[W2] + j)
                else:
                    sp.wait_ge(q_done, 2 + 2 * (D // P))
                for g in range(NKV):
                    dst = raw[W2][g * HEAD:(g + 1) * HEAD, :].rearrange("p (t n) -> p t n", t=2)
                    lo = g * 512 + j * 2 * HEAD
                    src = b_w_o[0][lo:lo + 2 * HEAD, :].rearrange("(t p) n -> p t n", p=HEAD)
                    sp.dma_start(dst, src).then_inc(loaded[W2], 16)

            for j in range(Q_PAIRS):
                load_o(j)
            chunk = ffn(1)
            sp.wait_ge(s_norm, 3 * NKV * NCHUNK)
            sp.wait_ge(p_full, NKV * NCHUNK)
            chunk(0)
            sp.wait_ge(prep, NCHUNK)
            norm_loads(3)
            norm(3)
            with sp.Fori(1, FFN_CHUNKS) as c:
                chunk(c)
            for par in range(2):
                sp.wait_ge(h_stored[par], 16 * (TT // 2) * 3)
            norm_loads(4)
            norm(4)
            for par in range(2):
                sp.wait_ge(h_stored[par], 16 * (TT // 2) * 4)

        @block.gpsimd
        def _(pool):
            total = {"gain": 0, "split": 0}

            def body(i, rounds, uses):
                gains, done = KT * sum(u[3] is not None for u in uses), 0
                for n, (s, use, data, gain, free) in enumerate(uses):
                    pool.wait_ge(*data)
                    if gain is not None:
                        pool.nop(nofuse=True)
                        for k in range(KT):
                            r = raw[s][:, k * PAIR:(k + 1) * PAIR]
                            nc.gpsimd.tensor_scalar(r, r, cols[:, gain + k:gain + k + 1], 0.0, ALU.mult, ALU.add).then_inc(gain_step, 1)
                        done += KT
                        pool.wait_ge(gain_step, i * gains + (total["gain"] + done))
                    if free is not None:
                        pool.wait_ge(*free)
                    pool.nop(nofuse=True)
                    nc.gpsimd.tensor_scalar(WH[s][:, :], raw[s][:, :], 1.0, 0.0, ALU.mult, ALU.add).then_inc(split_step, 1)
                    pool.wait_ge(split_step, i * len(uses) + (total["split"] + n + 1))
                    nc.gpsimd.tensor_tensor(WL[s][:, :], raw[s][:, :], f(WH[s][:, :]), ALU.subtract).then_inc(w_ready[s], 1)
                total["gain"] += gains * rounds
                total["split"] += len(uses) * rounds

            nc.gpsimd.memset(ident[:, :], 0.0).then_inc(pool_step, 1)
            pool.wait_ge(pool_step, 1)
            nc.gpsimd.affine_select(out=ident[:, :], in_=ident[:, :], compare_op=ALU.not_equal, fill=1.0,
                                    base=0, pattern=[[-1, P]], channel_multiplier=1).then_inc(ident_done, 1)
            nc.gpsimd.memset(acc[:, :, :].rearrange("p m n -> p (m n)"), 0.0).then_inc(acc_zero, TT)

            pool.wait_ge(tr_free, 1)
            gm = GAIN_MIX[0]
            body(0, 1, [(s, 0, (loaded[s], 16), gm, None) for s in (G, W2)])
            with pool.Fori(0, V_TILES // 4 - 1) as i:
                body(i, V_TILES // 4 - 1, [(s, i + 1, (loaded[s], i * 16 + 32), gm, (proj_full, i * 8 + v))
                                           for s, v in ((G, 4), (W2, 8))])

            def gmlp(g, frees):
                return [(G, g + USE_GMLP[G], (loaded[G], (g + USE_GMLP[G]) * 16 + 16), gm, frees[0]),
                        (U, g, (normed_v, g + 1), None, frees[1]),
                        (W2, g + USE_GMLP[W2], (loaded[W2], (g + USE_GMLP[W2]) * 16 + 16), None, frees[2])]
            body(0, 1, gmlp(0, ((proj_full, 2 * V_TILES - 4), None, (proj_full, 2 * V_TILES))))
            with pool.Fori(0, GMLP_CHUNKS - 1) as i:
                body(i, GMLP_CHUNKS - 1, gmlp(i + 1, ((act_full, i * 4 + 4), (mul_full, i * 4 + 4),
                                                      (down_full, i * 2 * DOWN_BANKS + 2 * DOWN_BANKS))))

            loads_ffn0 = (USE_FFN0[G], 3 * GMLP_CHUNKS, USE_FFN0[W2])
            loads_kv = tuple(n + FFN_CHUNKS for n in loads_ffn0)
            loads_q = (loads_kv[0] + 1, loads_kv[1], loads_kv[2])
            loads_o = (loads_q[0] + 2 * Q_PAIRS, loads_q[1] + 2 * Q_PAIRS, loads_q[2])
            loads_ffn1 = (loads_o[0], loads_o[1], loads_o[2] + 2 * Q_PAIRS)

            def zero_acc(n):
                for m in range(TT):
                    pool.wait_ge(h_new, TT * (n - 1) + m + 1)
                    nc.gpsimd.memset(acc[:, m, :], 0.0).then_inc(acc_zero, 1)

            def ffn(layer, n, before):
                use, loads = ((USE_FFN0, loads_ffn0), (USE_FFN1, loads_ffn1))[layer]
                st, dn, gain = STAGE_FFN[layer], (DOWN_FFN0, DOWN_FFN1)[layer], GAIN_FFN[layer]

                def uses(c, frees):
                    return [(s, c + use[s], (loaded[s], c * 16 + 16 * (loads[s] + 1)), g, frees[s])
                            for s, g in ((G, gain), (U, gain), (W2, None))]
                body(0, 1, uses(0, before))
                zero_acc(n)
                with pool.Fori(0, FFN_CHUNKS - 1) as i:
                    body(i, FFN_CHUNKS - 1, uses(i + 1, ((act_full, i * 4 + (2 * st + 4)), (mul_full, i * 4 + (2 * st + 4)),
                                                         (down_full, i * 2 * DOWN_BANKS + (dn + 2) * DOWN_BANKS))))

            ffn(0, 1, ((act_full, 2 * STAGE_FFN[0]), (mul_full, 2 * STAGE_FFN[0]), (down_full, DOWN_BANKS * DOWN_FFN0)))
            end_ffn0 = 2 * STAGE_FFN[1]
            body(0, 1, [(G, USE_KV[G], (loaded[G], 16 * (loads_kv[G] + 1)), GAIN_KV, (act_full, end_ffn0))])
            for j in range(Q_PAIRS):
                s = (U, G)[j % 2]
                free = (mul_full, end_ffn0) if j == 0 else (proj_full, PROJ_Q + 4 * (j - 1))
                body(0, 1, [(s, USE_Q[s] + j // 2, (loaded[s], 16 * (loads_q[s] + 4 * (j // 2 + 1))), GAIN_MIX[1], free)])

            pool.wait_ge(q_done, 2 + 2 * (D // P))
            pool.wait_ge(v_copied, 2)

            def prepare(n, par, m):
                first = isinstance(n, int)
                if not first:
                    wait_apart(pool, o_full, n * NKV - NKV)
                if par:
                    parts = [(kcH[1], kcL[1], kT[:, ds(m * P, P)]), (vcH[1], vcL[1], vt[:, ds(m, 1), :])]
                else:
                    parts = [(kcH[0][:, 0:CHUNK], kcL[0][:, 0:CHUNK], kT[:, ds(n * CHUNK, CHUNK)]),
                             (vcH[0], vcL[0], vshift[:, ds(m, 1), :])]
                    if not first:
                        parts.append((kcH[0][:, CHUNK:P], kcL[0][:, CHUNK:P], kT[:, ds(n * CHUNK - CHUNK, CHUNK)]))
                parts = [(h, l, src if len(src.shape) == 2 else src.rearrange("p a n -> p (a n)")) for h, l, src in parts]
                parts.append((qcH[par], qcL[par], qT[:, :, ds(n * CHUNK, CHUNK)]))
                for hi, lo, src in parts:
                    op = nc.gpsimd.tensor_copy(hi, src)
                op.then_inc(prep_hi, 1)
                wait_apart(pool, prep_hi, n + 1)
                for hi, lo, src in parts:
                    op = nc.gpsimd.tensor_tensor(lo, src, f(hi), ALU.subtract)
                op.then_inc(prep, 1)

            prepare(0, 0, 0)
            prepare(1, 1, 0)
            with pool.Fori(1, NCHUNK // 2) as m:
                prepare(m * 2, 0, m)
                prepare(m * 2 + 1, 1, m)

            for j in range(Q_PAIRS):
                body(0, 1, [(W2, USE_O[W2] + j, (loaded[W2], 16 * (loads_o[W2] + 2 * (j + 1))), None,
                             (down_full, DOWN_BANKS * (DOWN_O + 2 * j)))])
            ffn(1, 3, ((o_full, NKV * NCHUNK), (o_full, NKV * NCHUNK), (down_full, DOWN_BANKS * DOWN_FFN1)))

        @block.tensor
        def _(pe):
            def pair3(dst, wh, wl, xh, xl, first, last):
                nc.tensor.matmul(dst, wh, xh, start=first, stop=False)
                nc.tensor.matmul(dst, wh, xl, start=False, stop=False)
                return nc.tensor.matmul(dst, wl, xh, start=False, stop=last)

            def project(dst, s, tile, b, half):
                wh, wl = tile(WH[s], b), tile(WL[s], b)
                for k in range(KT):
                    t = slice(half * HALF, (half + 1) * HALF)
                    mm = pair3(dst, wh(k), wl(k), XH[:, k, t], XL[:, k, t], k == 0, k == KT - 1)
                return mm

            def down(n, half_of_x=None, x_pair=None):
                for m in range(4):
                    for o in range(2):
                        q = m * 2 + o
                        if not (isinstance(n, int) and n * DOWN_BANKS + q < 2):
                            pe.wait_ge(down_added, n * DOWN_BANKS + (q - 1))
                        dst = bank[4 + q % 2][:, :]
                        for t in range(2):
                            if x_pair is None:
                                lh, ll = hidH[:, t, m * P:(m + 1) * P], hidL[:, t, m * P:(m + 1) * P]
                            else:
                                tok = slice(half_of_x * HALF + m * P, half_of_x * HALF + (m + 1) * P)
                                lh, ll = XH[:, x_pair + t, tok], XL[:, x_pair + t, tok]
                            c = slice(t * D + o * HALF, t * D + (o + 1) * HALF)
                            nc.tensor.matmul(dst, lh, WH[W2][:, c], start=(t == 0), stop=False)
                            nc.tensor.matmul(dst, lh, WL[W2][:, c], start=False, stop=False)
                            mm = nc.tensor.matmul(dst, ll, WH[W2][:, c], start=False, stop=(t == 1))
                        mm.then_inc(down_full, 1)

            def transposes(src, dst):
                for q in range(4):
                    mm = nc.tensor.transpose(dst[:, q * P:(q + 1) * P], src[:, q * P:(q + 1) * P], ident[:, :])
                return mm

            def norm(n):
                def tile(m):
                    pe.wait_ge(rt_ready, m + (TT * n + 1))
                    for q in range(2):
                        before = m * 2 + (TR_NORM(n) + q - 1)
                        pe.wait_ge(tr_free, max(before, TR_COLS) if isinstance(m, int) else before)
                        transposes(rt[:, q * HALF:(q + 1) * HALF], bank[6 + q]).then_inc(tr_full, 1)
                tile(0)
                with pe.Fori(1, TT) as m:
                    tile(m)

            def x_ready(n):
                pe.wait_ge(tr_free, TR_NORM(n) + 2 * TT)

            def stage_ins(stage, half, s, full, first_bank):
                free = act_ready if first_bank == 0 else prod_ready
                for b in range(2):
                    if not (isinstance(stage, int) and stage == 0):
                        pe.wait_ge(free, stage * 2 + (b - 1))
                    project(bank[first_bank + b][:, :], s, in_tile, b, half).then_inc(full, 1)

            def hidden_ready(stage):
                pe.wait_ge(hid_hi, stage * 2 + 2)
                pe.wait_ge(hid_lo, stage * 2 + 2)

            def mix(stage, group, half):
                v = lambda t: t[:, :].rearrange("p (m d) -> p m d", m=TT)
                vh, vl = v(WH[U]), v(WL[U])
                wg = lambda t: t[:, ds(group, 1), :].rearrange("p a i -> p (a i)")
                for b in range(2):
                    if not (isinstance(stage, int) and stage == 0):
                        pe.wait_ge(prod_ready, stage * 2 + (b - 1))
                    for q in range(4):
                        m = half * 4 + q
                        dst = bank[2 + b][:, q * P:(q + 1) * P]
                        d = slice(b * P, (b + 1) * P)
                        mm = pair3(dst, vh[:, m, d], vl[:, m, d], wg(wsH), wg(wsL), True, True)
                    mm.then_inc(mul_full, 1)

            def ffn_chunk(layer, c, first):
                use = (USE_FFN0, USE_FFN1)[layer]
                base, dbase = STAGE_FFN[layer], (DOWN_FFN0, DOWN_FFN1)[layer]
                for h in range(2):
                    st = c * 2 + (base + h)
                    if h == 0:
                        pe.wait_ge(w_ready[G], c + (use[G] + 1))
                    stage_ins(st, h, G, act_full, 0)
                    if not (first and h == 0):
                        down_step(c * 2 + (base + h - 1), c * 2 + (dbase + h - 1), use, c, h)
                    if h == 0:
                        pe.wait_ge(w_ready[U], c + (use[U] + 1))
                    stage_ins(st, h, U, mul_full, 2)

            def down_step(stage, n, use, c, h):
                hidden_ready(stage)
                if h == 1:
                    pe.wait_ge(w_ready[W2], c + (use[W2] + 1))
                down(n)

            def gmlp_chunk(g, first):
                for h in range(2):
                    st = g * 2 + h
                    if h == 0:
                        pe.wait_ge(w_ready[G], g + (USE_GMLP[G] + 1))
                    stage_ins(st, h, G, act_full, 0)
                    if not (first and h == 0):
                        down_step(g * 2 + (h - 1), g * 2 + (h - 1), USE_GMLP, g, h)
                    if h == 0:
                        pe.wait_ge(w_ready[U], g + 1)
                    mix(st, g, h)

            pe.wait_ge(consts, 16 * 6)
            pe.wait_ge(ident_done, 1)
            nc.tensor.transpose(bank[6][:, 0:NCOLS], sg[0:NCOLS, 0, 0:P], ident[0:NCOLS, 0:NCOLS]).then_inc(tr_full, 1)
            norm(0)
            pe.wait_ge(ws_masked, 1)
            for q in range(2):
                pe.wait_ge(tr_free, TR_WS + q - 1)
                transposes(gpost[:, q * HALF:(q + 1) * HALF], bank[6 + q]).then_inc(tr_full, 1)
            pe.wait_ge(tr_free, TR_WS + 2)

            def v_back(idx, par):
                pe.wait_ge(v_act, idx + 1)
                if not (isinstance(idx, int) and idx < 2):
                    pe.wait_ge(vtr_free, idx - 1)
                transposes(sg[:, par, :], bank[6 + par]).then_inc(vtr_full, 1)

            def v_pair(i, s, e, first):
                pe.wait_ge(w_ready[s], i + 1)
                for b in range(2):
                    for h in range(2):
                        q = 4 * e + 2 * b + h
                        idx = i * 8 + q
                        if not (first and q < 4):
                            pe.wait_ge(v_act, idx - 3)
                        mm = project(bank[(2 * b + h)][:, :], s, in_tile, b, h)
                        mm.then_inc(proj_full, 1)
                        if not (first and q == 0):
                            v_back(idx - 1, (q - 1) % 2)

            for e, s in enumerate((G, W2)):
                v_pair(0, s, e, True)
            with pe.Fori(1, V_TILES // 4) as i:
                for e, s in enumerate((G, W2)):
                    v_pair(i, s, e, False)
            v_back(2 * V_TILES - 1, 1)

            pe.wait_ge(v_act, 2 * V_TILES)
            gmlp_chunk(0, True)
            with pe.Fori(1, GMLP_CHUNKS) as g:
                gmlp_chunk(g, False)
            down_step(STAGE_FFN[0] - 1, DOWN_FFN0 - 1, None, None, 0)

            def ffn(layer, n):
                norm(n)
                x_ready(n)
                ffn_chunk(layer, 0, True)
                with pe.Fori(1, FFN_CHUNKS) as c:
                    ffn_chunk(layer, c, False)
                down_step(STAGE_FFN[layer] + 2 * FFN_CHUNKS - 1,
                          (DOWN_FFN0, DOWN_FFN1)[layer] + 2 * FFN_CHUNKS - 1, None, None, 0)

            ffn(0, 1)
            norm(2)
            x_ready(2)
            pe.wait_ge(w_ready[G], USE_KV[G] + 1)
            for h in range(2):
                project(bank[h][:, :], G, in_tile, 0, h).then_inc(proj_full, 1)
            wv = [t[:, :].rearrange("p (k f) -> p k f", k=KT) for t in (WH[G], WL[G])]
            for h in range(2):
                for q in range(4):
                    tok = slice((h * 4 + q) * P, (h * 4 + q + 1) * P)
                    dst = bank[2 + h][:, q * P:(q + 1) * P]
                    for k in range(KT):
                        nc.tensor.matmul(dst, XH[:, k, tok], wv[0][:, k, P:PAIR], start=(k == 0), stop=False)
                        nc.tensor.matmul(dst, XH[:, k, tok], wv[1][:, k, P:PAIR], start=False, stop=False)
                        mm = nc.tensor.matmul(dst, XL[:, k, tok], wv[0][:, k, P:PAIR], start=False, stop=(k == KT - 1))
                mm.then_inc(proj_full, 1)
            for j in range(Q_PAIRS):
                s = (U, G)[j % 2]
                pe.wait_ge(w_ready[s], USE_Q[s] + j // 2 + 1)
                for b in range(2):
                    for h in range(2):
                        q = 4 * j + 2 * b + h
                        if q in (2, 3):
                            pe.wait_ge(v_copied, q - 1)
                        else:
                            pe.wait_ge(q_copied, q + 1 if q < 2 else q - 1)
                        project(bank[2 * b + h][:, :], s, in_tile, b, h).then_inc(proj_full, 1)

            def scores(n, par, kv, first_unit, keys):
                u = n * NKV + kv
                if kv == 0:
                    pe.wait_ge(prep, n + 1)
                if not first_unit:
                    pe.wait_ge(s_exp, u - 1)
                rows = slice(kv * HEAD, (kv + 1) * HEAD)
                for j in range(NPAIR):
                    q = slice(2 * j, 2 * j + 2)
                    mm = pair3(bank[kv][:, j * P:j * P + keys], qcH[par][rows, q, :], qcL[par][rows, q, :],
                               kcH[par][rows, 0:keys], kcL[par][rows, 0:keys], True, True)
                mm.then_inc(s_full, 1)

            def probs_back(n, kv, first_unit):
                u = n * NKV + kv
                pe.wait_ge(s_norm, u * 3 + 3)
                if not first_unit:
                    pe.wait_ge(p_lo, u - 1)
                for j in range(NPAIR):
                    mm = nc.tensor.transpose(bank[6 + kv][:, j * P:(j + 1) * P], prob[kv][:, j, :], ident[:, :])
                mm.then_inc(p_full, 1)

            def values(n, par, kv, first_unit):
                u = n * NKV + kv
                pe.wait_ge(p_hi, u + 1)
                pe.wait_ge(p_lo, u + 1)
                if not first_unit:
                    pe.wait_ge(o_lo, u - 1)
                pair3(bank[2 + kv][:, :], vcH[par], vcL[par], pTH[kv], pTL[kv], True, True).then_inc(o_full, 1)

            pe.wait_ge(q_done, 2 + 2 * (D // P))
            scores(0, 0, 0, True, CHUNK)
            scores(0, 0, 1, True, CHUNK)

            def attend(n, par, first, last):
                for kv in range(NKV):
                    probs_back(n, kv, first)
                    if not last:
                        scores(n + 1, 1 - par, kv, False, P)
                for kv in range(NKV):
                    values(n, par, kv, first)

            attend(0, 0, True, False)
            with pe.Fori(0, NCHUNK // 2 - 1) as i:
                attend(i * 2 + 1, 1, False, False)
                attend(i * 2 + 2, 0, False, False)
            attend(NCHUNK - 1, 1, False, True)

            pe.wait_ge(o_lo, NKV * NCHUNK)
            for j in range(Q_PAIRS):
                pe.wait_ge(w_ready[W2], USE_O[W2] + j + 1)
                for h in range(2):
                    down(DOWN_O + 2 * j + h, half_of_x=h, x_pair=2 * j)
            ffn(1, 3)

        @block.scalar
        def _(act):
            def norm_phase(n):
                post, pre = n > 0, n < 4
                if post:
                    act.wait_ge(down_added, DOWN_BANKS * (DOWN_FFN0, DOWN_O, DOWN_FFN1, DOWN_END)[n - 1])
                base_step = STEP_BASE[n]

                def step(k, par, has1, has2, has3):
                    one, two = has1 and post, has2 and pre
                    if one or two:
                        if not (isinstance(k, int) and k + base_step <= 0):
                            wait_apart(act, ms_done, k + base_step)
                    if one:
                        op = nc.scalar.activation(junk[:, 0, :], acc[:, ds(k, 1), :].rearrange("p a n -> p (a n)"),
                                                  ACT.Square, accum_out=ssq[:, 0:1])
                    if two:
                        other = 1 - par
                        if post:
                            act.wait_ge(h_new, k + TT * (n - 1))
                            src = hout[:, other, :]
                        else:
                            act.wait_ge(h_loaded[other], (k - 1 - other) * 8 + 16)
                            src = hin[:, other, :]
                        op = nc.scalar.activation(junk[:, 1, :], src, ACT.Square, accum_out=ssq[:, 1:2])
                    if one or two:
                        op.then_inc(sq_done, 1)
                        c = slice(0 if one else 1, 2 if two else 1)
                        act.wait_ge(ms_done, k + (base_step + 1))
                        nc.scalar.activation(root[:, c], rms[:, c], ACT.Sqrt).then_inc(root_done, 1)
                    if has3 and pre:
                        m = k - 2
                        for q in range(2):
                            wait_apart(act, tr_full, m * 2 + (TR_NORM(n) + q + 1))
                            nc.scalar.activation(XH[:, 4 * q:4 * q + 4, ds(m * P, P)],
                                                 bank[6 + q][:, :].rearrange("p (k t) -> p k t", k=4),
                                                 ACT.Copy).then_inc(tr_hi, 1)

                if pre:
                    step(0, 0, True, False, False)
                    step(1, 1, True, True, False)
                    with act.Fori(1, TT // 2) as j:
                        step(j * 2, 0, True, True, True)
                        step(j * 2 + 1, 1, True, True, True)
                    step(TT, 0, False, True, True)
                    step(TT + 1, 1, False, False, True)
                else:
                    step(0, 0, True, False, False)
                    with act.Fori(1, TT) as k:
                        step(k, 0, True, False, False)

            norm_phase(0)
            for q in range(2):
                act.wait_ge(tr_full, TR_WS + q + 1)
                nc.scalar.activation(wsH[:, 4 * q:4 * q + 4, :], bank[6 + q][:, :].rearrange("p (g i) -> p g i", g=4),
                                     ACT.Copy).then_inc(tr_hi, 1)

            def v_gelu(i, q, first):
                idx = i * 8 + q
                act.wait_ge(proj_full, idx + 1)
                if not (first and q < 2):
                    act.wait_ge(vtr_full, idx - 1)
                act.nop(nofuse=True)
                nc.scalar.activation(sg[:, q % 2, :], bank[q % 4][:, :], ACT.Gelu_apprx_tanh,
                                     bias=cols[:, ds(i * 4 + (BIAS_IN + V_TILES + q // 2), 1)]).then_inc(v_act, 1)

            for q in range(8):
                v_gelu(0, q, True)
            with act.Fori(1, V_TILES // 4) as i:
                for q in range(8):
                    v_gelu(i, q, False)
            act.wait_ge(v_stat, 2)
            nc.scalar.activation(vrstd[:, :], vrstd[:, :], ACT.Sqrt).then_inc(v_root, 1)

            def stage(st, func, bias, first=False):
                for b in range(2):
                    act.wait_ge(act_full, st * 2 + (b + 1))
                    if not first:
                        act.wait_ge(hid_lo, st * 2 + (b - 1))
                    act.nop(nofuse=True)
                    if bias is None:
                        nc.scalar.activation(sg[:, b, :], bank[b][:, :], func).then_inc(act_ready, 1)
                    else:
                        nc.scalar.activation(sg[:, b, :], bank[b][:, :], func, bias=bias(b)).then_inc(act_ready, 1)

                for b in range(2):
                    act.wait_ge(prod_ready, st * 2 + (b + 1))
                    nc.scalar.activation(hidH[:, b, :], sg[:, b, :], ACT.Copy).then_inc(hid_hi, 1)

            def gmlp(g, first):
                for h in range(2):
                    stage(g * 2 + h, ACT.Gelu_apprx_tanh, lambda b: cols[:, ds(g * 2 + (BIAS_IN + b), 1)], first and h == 0)

            act.wait_ge(vtr_full, 2 * V_TILES)
            gmlp(0, True)
            with act.Fori(1, GMLP_CHUNKS) as g:
                gmlp(g, False)

            def ffn(layer):
                with act.Fori(0, 2 * FFN_CHUNKS) as c:
                    stage(c + STAGE_FFN[layer], ACT.Silu, None)

            norm_phase(1)
            ffn(0)
            norm_phase(2)

            def plain_and_rotated(r, full, src):
                e = r % 2
                act.wait_ge(proj_full, full)
                if r >= 2:
                    act.wait_ge(q_done, r - 1)
                nc.scalar.activation(qplain[e], src[:, :], ACT.Copy)
                for q in range(4):
                    a, b = q * 32, (q ^ 1) * 32
                    op = nc.scalar.activation(qrot[e][a:a + 32, :], src[b:b + 32, :], ACT.Copy)
                op.then_inc(q_copied, 1)

            for h in range(2):
                plain_and_rotated(h, PROJ_KV + h + 1, bank[h])
            for h in range(2):
                act.wait_ge(proj_full, PROJ_KV + 3 + h)
                src = bank[2 + h][:, :].rearrange("p (m d) -> p m d", m=4)
                after = min(4, TT - 1 - 4 * h)
                nc.scalar.activation(vshift[0:CHUNK, 4 * h:4 * h + 4, :], src[0:CHUNK], ACT.Copy)
                nc.scalar.activation(vshift[CHUNK:P, 4 * h + 1:4 * h + 1 + after, :], src[CHUNK:P, 0:after, :], ACT.Copy)
                nc.scalar.activation(vt[:, 4 * h:4 * h + 4, :], src, ACT.Copy).then_inc(v_copied, 1)
            for q in range(2 * (D // P)):
                plain_and_rotated(2 + q, PROJ_Q + q + 1, bank[q % 4])

            def exps(n, kv, keys, first):
                u = n * NKV + kv
                act.wait_ge(s_max, u * 4 + 4)
                if not first:
                    act.wait_ge(p_full, u - 1)
                nc.scalar.activation(a_snk[:, kv, :], a_off[:, kv, :], ACT.Exp)
                for j in range(NPAIR):
                    op = nc.scalar.activation(prob[kv][:, j, 0:keys], bank[kv][:, j * P:j * P + keys], ACT.Exp,
                                              bias=a_neg[:, kv, j:j + 1], scale=SCALE, accum_out=a_sum[:, kv, j:j + 1])
                op.then_inc(s_exp, 1)

            def p_split(n, kv, first):
                u = n * NKV + kv
                act.wait_ge(p_full, u + 1)
                if not first:
                    act.wait_ge(o_full, u - 1)
                nc.scalar.activation(pTH[kv], bank[6 + kv][:, :], ACT.Copy).then_inc(p_hi, 1)

            def o_split(n, kv):
                u = n * NKV + kv
                wait_apart(act, o_full, u + 1)
                r = slice(kv * HEAD, (kv + 1) * HEAD)
                nc.scalar.activation(XH[r, :, ds(n * CHUNK, CHUNK)],
                                     bank[2 + kv][r, :].rearrange("p (t c) -> p t c", t=KT), ACT.Copy).then_inc(o_hi, 1)

            def attend(n, keys, first, last):
                for kv in range(NKV):
                    p_split(n, kv, first)
                if not last:
                    for kv in range(NKV):
                        exps(n + 1, kv, P, False)
                for kv in range(NKV):
                    o_split(n, kv)

            act.wait_ge(q_done, 2 + 2 * (D // P))
            for kv in range(NKV):
                exps(0, kv, CHUNK, True)
            attend(0, None, True, False)
            with act.Fori(1, NCHUNK - 1) as n:
                attend(n, None, False, False)
            attend(NCHUNK - 1, None, False, True)
            norm_phase(3)
            ffn(1)
            norm_phase(4)

        @block.vector
        def _(dve):
            def norm_phase(n):
                post, pre = n > 0, n < 4
                base_step = STEP_BASE[n]
                rbase = TT * n
                if post:
                    dve.wait_ge(g_loaded, 16 * n)

                def step(k, par, has1, has2, has3):
                    one, two = has1 and post, has2 and pre
                    if one or two:
                        c = slice(0 if one else 1, 2 if two else 1)
                        dve.wait_ge(sq_done, k + (base_step + 1))
                        nc.vector.tensor_scalar(rms[:, c], ssq[:, c], 1.0 / D, EPS, ALU.mult, ALU.add).then_inc(ms_done, 1)
                        dve.wait_ge(root_done, k + (base_step + 1))
                        nc.vector.reciprocal(rstd[:, c], root[:, c]).then_inc(rstd_done, 1)
                        dve.wait_ge(rstd_done, k + (base_step + 1))
                    if two:
                        src = (hout if post else hin)[:, 1 - par, :]
                        dve.wait_ge(tr_full, k * 2 + (TR_NORM(n) - 2))
                        nc.vector.tensor_scalar(rt[:, :], src, rstd[:, 1:2], None, ALU.mult).then_inc(rt_ready, 1)
                    if one:
                        a = acc[:, ds(k, 1), :].rearrange("p a n -> p (a n)")
                        nc.vector.scalar_tensor_tensor(out=a, in0=a, scalar=rstd[:, 0:1], in1=gpost[:, :],
                                                       op0=ALU.mult, op1=ALU.mult).then_inc(scaled, 1)
                        dve.wait_ge(h_loaded[par], H_LOADS[n] + (k - par) * 8 + 16)
                        if n > 1 or not isinstance(k, int) or k > 1:
                            dve.wait_ge(h_stored[par], (k - par) * 8 + 16 * (TT // 2) * (n - 1))
                        dve.wait_ge(scaled, k + (TT * (n - 1) + 1))
                        nc.vector.tensor_tensor(hout[:, par, :], hin[:, par, :], a, ALU.add).then_inc(h_new, 1)
                    if has3 and pre:
                        m = k - 2
                        for q in range(2):
                            dve.wait_ge(tr_hi, m * 2 + (TR_NORM(n) + q))
                            nc.vector.tensor_tensor(XL[:, 4 * q:4 * q + 4, ds(m * P, P)],
                                                    bank[6 + q][:, :].rearrange("p (k t) -> p k t", k=4),
                                                    f(XH[:, 4 * q:4 * q + 4, ds(m * P, P)]), ALU.subtract).then_inc(tr_free, 1)

                if pre:
                    step(0, 0, True, False, False)
                    step(1, 1, True, True, False)
                    with dve.Fori(1, TT // 2) as j:
                        step(j * 2, 0, True, True, True)
                        step(j * 2 + 1, 1, True, True, True)
                    step(TT, 0, False, True, True)
                    step(TT + 1, 1, False, False, True)
                else:
                    step(0, 0, True, False, False)
                    step(1, 1, True, False, False)
                    with dve.Fori(1, TT // 2) as j:
                        step(j * 2, 0, True, False, False)
                        step(j * 2 + 1, 1, True, False, False)

            dve.wait_ge(tr_full, 1)
            nc.vector.tensor_copy(cols[:, :], bank[6][:, 0:NCOLS]).then_inc(tr_free, 1)
            norm_phase(0)
            dve.wait_ge(ws_loaded, 16)
            nc.vector.memset(gpost[0:CHUNK, :].rearrange("p (g j) -> p g j", g=GROUPS)[:, :, CHUNK:P], 0.0).then_inc(ws_masked, 1)
            for q in range(2):
                dve.wait_ge(tr_hi, TR_WS + q)
                nc.vector.tensor_tensor(wsL[:, 4 * q:4 * q + 4, :], bank[6 + q][:, :].rearrange("p (g i) -> p g i", g=4),
                                        f(wsH[:, 4 * q:4 * q + 4, :]), ALU.subtract).then_inc(tr_free, 1)

            vg = raw[U][:, :].rearrange("p (m d) -> p m d", m=TT)

            def v_copy(i, q, first):
                idx = i * 8 + q
                dve.wait_ge(vtr_full, idx + 1)
                h, b = q % 2, (q // 2) % 2
                if q % 4 == 0 and not (first and q == 0):
                    dve.wait_ge(v_parked, i * 32 + 4 * q)
                src = bank[6 + q % 2][:, :].rearrange("p (m d) -> p m d", m=4)
                for m in range(4):
                    nc.vector.bn_stats(stats[:, 4 * h + m, ds(i * 4 + q // 2, 1), :].rearrange("p a s -> p (a s)"), src[:, m, :])
                nc.vector.tensor_copy(vg[:, 4 * h:4 * h + 4, b * P:(b + 1) * P], src).then_inc(vtr_free, 1)

            for q in range(8):
                v_copy(0, q, True)
            with dve.Fori(1, V_TILES // 4) as i:
                for q in range(8):
                    v_copy(i, q, False)
            dve.wait_ge(vtr_free, 2 * V_TILES)
            for m in range(TT):
                op = nc.vector.bn_aggr(vmean[:, m, :], stats[:, m, :, :].rearrange("p a s -> p (a s)"))
            op.then_inc(v_stat, 1)
            dve.wait_ge(v_stat, 1)
            nc.vector.tensor_scalar(vrstd[:, :], vmean[:, :, 1], EPS, None, ALU.add).then_inc(v_stat, 1)
            dve.wait_ge(v_root, 1)
            nc.vector.reciprocal(vrstd[:, :], vrstd[:, :]).then_inc(v_stat, 1)
            dve.wait_ge(v_stat, 3)

            def layer_norm(g):
                dve.wait_ge(loaded[U], g * 48 + 48)
                for m in range(TT):
                    op = nc.vector.tensor_scalar(vg[:, m, :], vg[:, m, :], vmean[:, m, 0:1], vrstd[:, m:m + 1],
                                                 ALU.subtract, ALU.mult)
                op.then_inc(ln_step, 1)
                dve.wait_ge(ln_step, g * 2 + 1)
                lg = lambda e: lngb[:, e:e + 1, :].to_broadcast([P, TT, PAIR])
                nc.vector.tensor_tensor(vg, vg, lg(0), ALU.mult).then_inc(ln_step, 1)
                dve.wait_ge(ln_step, g * 2 + 2)
                nc.vector.tensor_tensor(vg, vg, lg(1), ALU.add).then_inc(normed_v, 1)

            def add_down(n, copy=False, half=0):
                for m in range(4):
                    for o in range(2):
                        q = m * 2 + o
                        dve.wait_ge(down_full, n * DOWN_BANKS + (q + 1))
                        a = acc[:, 4 * half + m, o * HALF:(o + 1) * HALF]
                        if copy:
                            nc.vector.tensor_copy(a, bank[4 + q % 2][:, :]).then_inc(down_added, 1)
                        else:
                            nc.vector.tensor_tensor(a, bank[4 + q % 2][:, :], a, ALU.add).then_inc(down_added, 1)

            def hidden_lo(st, b):
                dve.wait_ge(hid_hi, st * 2 + (b + 1))
                nc.vector.tensor_tensor(hidL[:, b, :], sg[:, b, :], f(hidH[:, b, :]), ALU.subtract).then_inc(hid_lo, 1)

            def gmlp(g, first):
                for h in range(2):
                    st = g * 2 + h
                    if not (first and h == 0):
                        add_down(g * 2 + (h - 1), half=1 - h)
                    for b in range(2):
                        dve.wait_ge(mul_full, st * 2 + (b + 1))
                        mixed = bank[2 + b][:, :].rearrange("p (m i) -> p m i", m=4)
                        nc.vector.tensor_tensor(mixed, mixed, bs[:, ds(g, 1), :].to_broadcast([P, 4, P]), ALU.add).then_inc(bias_done, 1)
                        dve.wait_ge(bias_done, st * 2 + (b + 1))
                        dve.wait_ge(act_ready, st * 2 + (b + 1))
                        nc.vector.tensor_tensor(sg[:, b, :], bank[2 + b][:, :], sg[:, b, :], ALU.mult).then_inc(prod_ready, 1)
                    for b in range(2):
                        hidden_lo(st, b)

            layer_norm(0)
            dve.wait_ge(bs_loaded, 16)
            dve.wait_ge(acc_zero, TT)
            gmlp(0, True)
            with dve.Fori(1, GMLP_CHUNKS) as g:
                layer_norm(g)
                gmlp(g, False)
            add_down(DOWN_FFN0 - 1, half=1)

            def ffn(layer, zeroed):
                base, dbase = STAGE_FFN[layer], (DOWN_FFN0, DOWN_FFN1)[layer]
                dve.wait_ge(acc_zero, zeroed)

                def chunk(c, first):
                    for h in range(2):
                        st = c * 2 + (base + h)
                        if not (first and h == 0):
                            add_down(c * 2 + (dbase + h - 1), half=1 - h)
                        for b in range(2):
                            dve.wait_ge(mul_full, st * 2 + (b + 1))
                            dve.wait_ge(act_ready, st * 2 + (b + 1))
                            nc.vector.tensor_tensor(sg[:, b, :], bank[2 + b][:, :], sg[:, b, :], ALU.mult).then_inc(prod_ready, 1)
                        for b in range(2):
                            hidden_lo(st, b)

                chunk(0, True)
                with dve.Fori(1, FFN_CHUNKS) as c:
                    chunk(c, False)
                add_down(dbase + 2 * FFN_CHUNKS - 1, half=1)

            norm_phase(1)
            ffn(0, 2 * TT)
            norm_phase(2)

            def rotate(r, e, dst, half):
                t = slice(half * HALF, (half + 1) * HALF)
                dve.wait_ge(q_copied, r + 1)
                nc.vector.tensor_tensor(qplain[e], qplain[e], cosT[:, t], ALU.mult)
                nc.vector.tensor_tensor(qrot[e], qrot[e], sinT[:, t], ALU.mult).then_inc(rope_step, 1)
                dve.wait_ge(rope_step, r + 1)
                nc.vector.tensor_tensor(dst, qplain[e], qrot[e], ALU.add).then_inc(q_done, 1)

            nc.vector.memset(vshift[CHUNK:P, 0, :], 0.0)
            dve.wait_ge(rope_loaded, 32)
            for h in range(2):
                rotate(h, h, kT[:, h * HALF:(h + 1) * HALF], h)
            for q in range(2 * (D // P)):
                rotate(2 + q, q % 2, qT[:, q // 2, (q % 2) * HALF:(q % 2 + 1) * HALF], q % 2)

            def maxima(n, kv, keys):
                u = n * NKV + kv
                dve.wait_ge(s_full, u + 1)
                sc = bank[kv][:, :].rearrange("p (j m) -> p j m", j=NPAIR)[:, :, 0:keys]
                nc.vector.reduce_max(a_max[:, kv, :], sc, AX_X).then_inc(s_max, 1)
                dve.wait_ge(s_max, u * 4 + 1)
                nc.vector.scalar_tensor_tensor(out=a_max[:, kv, :], in0=a_max[:, kv, :], scalar=SCALE, in1=sink[:, kv, :],
                                               op0=ALU.mult, op1=ALU.max).then_inc(s_max, 1)
                dve.wait_ge(s_max, u * 4 + 2)
                nc.vector.tensor_scalar(a_neg[:, kv, :], a_max[:, kv, :], -1.0, None, ALU.mult).then_inc(s_max, 1)
                nc.vector.tensor_tensor(a_off[:, kv, :], sink[:, kv, :], a_max[:, kv, :], ALU.subtract).then_inc(s_max, 1)

            def normalise(n, kv):
                u = n * NKV + kv
                dve.wait_ge(s_exp, u + 1)
                nc.vector.tensor_tensor(a_den[:, kv, :], a_sum[:, kv, :], a_snk[:, kv, :], ALU.add).then_inc(s_norm, 1)
                dve.wait_ge(s_norm, u * 3 + 1)
                nc.vector.reciprocal(a_inv[:, kv, :], a_den[:, kv, :]).then_inc(s_norm, 1)
                dve.wait_ge(s_norm, u * 3 + 2)
                inv = a_inv[:, kv, :].unsqueeze(2).to_broadcast([P, NPAIR, P])
                nc.vector.tensor_tensor(prob[kv], prob[kv], inv, ALU.mult).then_inc(s_norm, 1)

            def p_rest(n, kv, first):
                u = n * NKV + kv
                dve.wait_ge(p_hi, u + 1)
                nc.vector.tensor_tensor(pTL[kv], bank[6 + kv][:, :], f(pTH[kv]), ALU.subtract).then_inc(p_lo, 1)

            def o_rest(n, kv):
                u = n * NKV + kv
                dve.wait_ge(o_hi, u + 1)
                r = slice(kv * HEAD, (kv + 1) * HEAD)
                nc.vector.tensor_tensor(XL[r, :, ds(n * CHUNK, CHUNK)], bank[2 + kv][r, :].rearrange("p (t c) -> p t c", t=KT),
                                        f(XH[r, :, ds(n * CHUNK, CHUNK)]), ALU.subtract).then_inc(o_lo, 1)

            def attend(n, last):
                for kv in range(NKV):
                    p_rest(n, kv, False)
                if not last:
                    for kv in range(NKV):
                        maxima(n + 1, kv, P)
                for kv in range(NKV):
                    o_rest(n, kv)
                if not last:
                    for kv in range(NKV):
                        normalise(n + 1, kv)

            dve.wait_ge(sink_loaded, 16 * 4)
            for kv in range(NKV):
                nc.vector.memset(prob[kv][:, :, CHUNK:P], 0.0)
                maxima(0, kv, CHUNK)
            for kv in range(NKV):
                normalise(0, kv)
            with dve.Fori(0, NCHUNK - 1) as n:
                attend(n, False)
            attend(NCHUNK - 1, True)

            for j in range(Q_PAIRS):
                for h in range(2):
                    add_down(DOWN_O + 2 * j + h, copy=(j == 0), half=h)
            norm_phase(3)
            ffn(1, 3 * TT)
            norm_phase(4)


STEPS = [TT, TT + 1, TT + 1, TT + 1, TT]
STEP_BASE = [sum(STEPS[:n]) for n in range(5)]
STEP_BASE[0] = -1
H_LOADS = [16 * (TT // 2) * n for n in range(5)]


def rope_tables():
    pos = np.arange(S, dtype=np.float32)
    inv = (np.float32(1.0) / (np.float32(10000.0) ** (np.arange(0, HEAD, 2, dtype=np.float32) / np.float32(HEAD)))).astype(np.float32)
    ang = (inv[:, None] * pos[None, :]).astype(np.float32)
    c, s = np.cos(ang).astype(np.float32), np.sin(ang).astype(np.float32)
    return np.concatenate([c] * 4, 0), np.concatenate([-s, s, -s, s], 0)


_INS = ["x", "norm_mix_pre", "norm_mix_post", "norm_ffn_pre", "norm_ffn_post", "a_w_in", "a_b_in", "a_ln_g", "a_ln_b",
        "a_w_s", "a_b_s", "a_w_out", "kv_norm", "w_kv", "b_w_q", "b_sinks", "b_w_o", "f_w_gate_up", "f_w_down"]


def kernel(**inputs):
    import concourse.bacc as bacc
    from concourse.bass_utils import run_bass_kernel_spmd

    nc = bacc.Bacc("TRN2", target_bir_lowering=False, num_devices=1)
    cos, sin = rope_tables()
    arrays, args = {}, []
    for name in _INS + ["rope_cos", "rope_sin"]:
        a = cos if name == "rope_cos" else sin if name == "rope_sin" else np.ascontiguousarray(inputs[name])
        arrays[f"in_{name}"] = a
        args.append(nc.dram_tensor(f"in_{name}", a.shape, mybir.dt.from_np(a.dtype), kind="ExternalInput").ap())
    y = nc.dram_tensor("out_y", [1, S, D], F32, kind="ExternalOutput").ap()
    build_trunk(nc, *args, y)
    r = run_bass_kernel_spmd(nc, [arrays], core_ids=[0])
    return r.results[0]["out_y"]
```

```python
import numpy as np

import concourse.bass as bass
from concourse import mybir
from concourse.alu_op_type import AluOpType as ALU

F32 = mybir.dt.float32
F32R = mybir.dt.float32r
ACT = mybir.ActivationFunctionType
AX_X = mybir.AxisListType.X
ds = bass.ds

P = 128
D = 1024
S = 1024
KT = D // P
TT = S // P
HALF = 512
GMLP_FFN = 4 * D
GMLP_HALF = GMLP_FFN // 2
GROUPS = 8
PAIR = 2 * P
assert GMLP_HALF // GROUPS == PAIR
D_FF = -(-8 * D // (3 * 256)) * 256
HEAD = 64
CHUNK = 64
NCHUNK = S // CHUNK
SCALE = 1.0 / float(np.sqrt(HEAD))
EPS = 1e-6
GMLP_CHUNKS = GMLP_HALF // PAIR
FFN_CHUNKS = D_FF // PAIR
V_TILES = GMLP_HALF // P
Q_PAIRS = D // PAIR
G, U, W2 = 0, 1, 2

GAIN_MIX = (0, 8)
GAIN_FFN = (16, 24)
GAIN_KV = 32
BIAS_IN = 40
NCOLS = BIAS_IN + GMLP_FFN // P

STAGE_GMLP = 0
STAGE_FFN = (2 * GMLP_CHUNKS, 2 * GMLP_CHUNKS + 2 * FFN_CHUNKS)
STAGES = STAGE_FFN[1] + 2 * FFN_CHUNKS
DOWN_GMLP = 0
DOWN_FFN0 = 2 * GMLP_CHUNKS
DOWN_O = DOWN_FFN0 + 2 * FFN_CHUNKS
DOWN_FFN1 = DOWN_O + 2 * Q_PAIRS
DOWN_END = DOWN_FFN1 + 2 * FFN_CHUNKS
DOWN_BANKS = 8
USE_V = (0, None, 0)
USE_GMLP = (V_TILES // 4, 0, V_TILES // 4)
USE_FFN0 = (USE_GMLP[0] + GMLP_CHUNKS, 0, USE_GMLP[2] + GMLP_CHUNKS)
USE_KV = tuple(u + FFN_CHUNKS for u in USE_FFN0)
USE_Q = (USE_KV[0] + 1, USE_KV[1], USE_KV[2])
USE_O = (USE_Q[0] + Q_PAIRS // 2, USE_Q[1] + Q_PAIRS // 2, USE_Q[2])
USE_FFN1 = (USE_O[0], USE_O[1] + Q_PAIRS // 2, USE_O[2] + Q_PAIRS // 2)
PROJ_V = 0
PROJ_KV = PROJ_V + 2 * V_TILES
PROJ_Q = PROJ_KV + 4
PROJ_END = PROJ_Q + 2 * (D // P)
TR_COLS = 1
TR_NORM = lambda n: TR_COLS + 2 * TT * n + (2 if n else 0)
TR_WS = TR_COLS + 2 * TT
O_ORDER = ((0, 0), (0, 1), (1, 0), (1, 1), (2, 0), (3, 0), (2, 1), (3, 1))
NKV = 2
NPAIR = 4


def wait_apart(eng, sem, value):
    eng.wait_ge(sem, value)
    eng.nop(nofuse=True)


def build_trunk(nc, x, norm_mix_pre, norm_mix_post, norm_ffn_pre, norm_ffn_post, a_w_in, a_b_in, a_ln_g,
                a_ln_b, a_w_s, a_b_s, a_w_out, kv_norm, w_kv, b_w_q, b_sinks, b_w_o, f_w_gate_up,
                f_w_down, rope_cos, rope_sin, out):
    KB = 1024
    place = {"at": -(-nc.sbuf_base // 64) * 64}

    def sb(name, shape, dtype=F32, at=None):
        size = int(np.prod(shape[1:])) * 4
        if at is None:
            at = place["at"]
            place["at"] = -(-(at + size) // 64) * 64
        t = nc.alloc_sbuf_tensor_at(name, list(shape), dtype, offset=at)
        return t

    here = lambda: place["at"]

    acc = sb("acc", [P, TT, D])
    XH = sb("XH", [P, KT, S], F32R)
    XL = sb("XL", [P, KT, S], F32R)
    at_w = here()
    WH = [sb(f"WH{s}", [P, 8 * PAIR], F32R) for s in range(3)]
    prob = [sb(f"prob{k}", [P, NPAIR, P], at=at_w + 2 * KB * k) for k in range(NKV)]
    pT = [sb(f"pT{k}", [P, HALF], at=at_w + 4 * KB + 2 * KB * k) for k in range(NKV)]
    qc = [sb(f"qc{e}", [P, KT * CHUNK], at=at_w + 24 * KB + 2 * KB * e) for e in range(2)]
    vc = [sb(f"vc{e}", [P, P], at=at_w + 28 * KB + KB * e) for e in range(2)]
    vn = sb("vn", [P, TT, PAIR], at=at_w + 8 * KB)
    cosT = sb("cosT", [P, S], at=at_w + 16 * KB)
    sinT = sb("sinT", [P, S], at=at_w + 20 * KB)
    WL = [sb(f"WL{s}", [P, 8 * PAIR], F32R) for s in range(3)]
    raw = [sb(f"raw{s}", [P, 8 * PAIR]) for s in range(3)]
    at_hid = here()
    hidH = sb("hidH", [P, 2, HALF], F32R)
    hidL = sb("hidL", [P, 2, HALF], F32R)
    stats = sb("stats", [P, TT, V_TILES, 6], at=at_hid)
    vshift = sb("vshift", [P, TT, P], at=at_hid)
    kz1 = sb("kz1", [P, S], at=at_hid + 4 * KB)
    sg = sb("sg", [P, 2, HALF])
    junk = sb("junk", [P, D])
    gpost = sb("gpost", [P, D])
    at_e = here()
    hin = sb("hin", [P, 2, D])
    hout = sb("hout", [P, 2, D])
    wsT = sb("wsT", [P, GROUPS, P], at=at_e)
    bs = sb("bs", [P, GROUPS, P], at=at_e + 8 * KB)
    lngb = sb("lngb", [P, 2, PAIR], at=at_e + 12 * KB)
    kz = [sb("kz0", [P, S], at=at_e), kz1]
    vt = sb("vt", [P, TT, P], at=at_e + 4 * KB)
    ident = sb("ident", [P, P])
    cols = sb("cols", [P, NCOLS])
    sink = sb("sink", [P, NKV, NPAIR])
    vmean = sb("vmean", [P, TT, 2])
    vrstd = sb("vrstd", [P, TT])
    ssq = sb("ssq", [P, 2])
    rms = sb("rms", [P, 2])
    root = sb("root", [P, 2])
    rstd = sb("rstd", [P, 2])
    a_max = sb("a_max", [P, NKV, NPAIR])
    neg_sink = sb("neg_sink", [P, NKV, NPAIR])
    a_neg = sb("a_neg", [P, NKV, NPAIR])
    a_off = sb("a_off", [P, NKV, NPAIR])
    a_snk = sb("a_snk", [P, NKV, NPAIR])
    a_sum = sb("a_sum", [P, NKV, NPAIR])
    a_den = sb("a_den", [P, NKV, NPAIR])
    a_inv = sb("a_inv", [P, NKV, NPAIR])
    qplain = [raw[2][:, e * 1024:e * 1024 + 512] for e in range(2)]
    qrot = [raw[2][:, e * 1024 + 512:(e + 1) * 1024] for e in range(2)]
    qT = acc[:, :, :].rearrange("p m n -> p (m n)")

    bank = [nc.alloc_psum_tensor(f"bank{b}", [P, HALF], F32) for b in range(8)]

    h_dram = [nc.dram_tensor(f"h{n}", [TT, P, D], F32, kind="Internal").ap() for n in range(1, 4)]
    v_dram = nc.dram_tensor("v_park", [GMLP_CHUNKS - 1, P, TT * PAIR], F32, kind="Internal").ap()
    x_in = x.rearrange("a (m p) d -> (a m) p d", p=P)
    out_t = out.rearrange("a (m p) d -> (a m) p d", p=P)
    h_from = [x_in, x_in, h_dram[0], h_dram[1], h_dram[2]]
    h_to = [None, h_dram[0], h_dram[1], h_dram[2], out_t]
    post_gain = [None, norm_mix_post[0:1, :], norm_ffn_post[0:1, :], norm_mix_post[1:2, :], norm_ffn_post[1:2, :]]

    sem = nc.alloc_semaphore
    loaded = [sem(f"loaded{s}") for s in range(3)]
    normed_v = sem("normed_v")
    w_ready = [sem(f"w_ready{s}") for s in range(3)]
    pool_step = sem("pool_step")
    proj_full = sem("proj_full")
    act_full = sem("act_full")
    act_ready = sem("act_ready")
    mul_full = sem("mul_full")
    prod_ready = sem("prod_ready")
    hid_hi = sem("hid_hi")
    hid_lo = sem("hid_lo")
    down_full = sem("down_full")
    down_added = sem("down_added")
    acc_zero = sem("acc_zero")
    tr_full = sem("tr_full")
    tr_hi = sem("tr_hi")
    tr_free = sem("tr_free")
    h_loaded = [sem(f"h_loaded{e}") for e in range(2)]
    h_stored = [sem(f"h_stored{e}") for e in range(2)]
    h_new = sem("h_new")
    g_loaded = sem("g_loaded")
    sq_done = sem("sq_done")
    ms_done = sem("ms_done")
    root_done = sem("root_done")
    rstd_done = sem("rstd_done")
    scaled = sem("scaled")
    rt_ready = sem("rt_ready")
    consts = sem("consts")
    ws_loaded = sem("ws_loaded")
    rope_loaded = sem("rope_loaded")
    ident_done = sem("ident_done")
    ws_masked = sem("ws_masked")
    sink_loaded = sem("sink_loaded")
    bs_loaded = sem("bs_loaded")
    gain_step = sem("gain_step")
    split_step = sem("split_step")
    v_act = sem("v_act")
    vtr_full = sem("vtr_full")
    vtr_free = sem("vtr_free")
    v_parked = sem("v_parked")
    v_stat = sem("v_stat")
    v_root = sem("v_root")
    ln_step = sem("ln_step")
    bias_done = sem("bias_done")
    q_copied = sem("q_copied")
    rope_step = sem("rope_step")
    q_done = sem("q_done")
    vT_copied = sem("vT_copied")
    v_copied = sem("v_copied")
    q_staged = sem("q_staged")
    v_staged = sem("v_staged")
    s_full = sem("s_full")
    s_max = sem("s_max")
    s_exp = sem("s_exp")
    s_norm = sem("s_norm")
    p_full = sem("p_full")
    p_copied = sem("p_copied")
    o_full = sem("o_full")
    o_hi = sem("o_hi")
    o_lo = sem("o_lo")

    def f(ap):
        return ap.bitcast(F32)

    def in_tile(t, b):
        v = t[:, :].rearrange("p (k f) -> p k f", k=KT)
        return lambda k: v[:, k, b * P:(b + 1) * P]

    with nc.Block() as block:
        @block.sync
        def _(sp):
            def load_in(s, use, src, first=False):
                if not first:
                    sp.wait_ge(w_ready[s], use)
                sp.dma_start(raw[s][:, :].rearrange("p (k f) -> p k f", k=KT),
                             src.rearrange("(k p) f -> p k f", p=P)).then_inc(loaded[s], 16)

            def load_down(use, src, first=False):
                if not first:
                    sp.wait_ge(w_ready[W2], use)
                sp.dma_start(raw[W2][:, :].rearrange("p (t n) -> p t n", t=2),
                             src.rearrange("(t p) n -> p t n", p=P)).then_inc(loaded[W2], 16)

            def norm_loads(n):
                if n:
                    sp.dma_start(gpost[:, :], post_gain[n].to_broadcast([P, D])).then_inc(g_loaded, 16)
                for m in range(2):
                    sp.dma_start(hin[:, m, :], h_from[n][m]).then_inc(h_loaded[m], 16)

            def norm_tile(n, m, par, more):
                if n:
                    sp.wait_ge(h_new, TT * (n - 1) + m + 1)
                    sp.dma_start(h_to[n][ds(m, 1)].rearrange("a p d -> (a p) d"), hout[:, par, :]).then_inc(h_stored[par], 16)
                else:
                    sp.wait_ge(rt_ready, m + 1)
                if more:
                    sp.dma_start(hin[:, par, :], h_from[n][ds(m + 2, 1)].rearrange("a p d -> (a p) d")).then_inc(h_loaded[par], 16)

            def norm(n, between=lambda: None, start=0):
                for m in range(start, TT // 2):
                    norm_tile(n, m, m % 2, True)
                between()
                with sp.Fori(TT // 4, TT // 2 - 1) as j:
                    for par in range(2):
                        norm_tile(n, j * 2 + par, par, True)
                for m in (TT - 2, TT - 1):
                    norm_tile(n, m, m % 2, False)

            def ffn(layer):
                use = (USE_FFN0, USE_FFN1)[layer]
                gu, down = f_w_gate_up[layer], f_w_down[layer]

                def chunk(c):
                    load_in(G, use[G] + c, gu[:, ds(c * PAIR, PAIR)])
                    load_in(U, use[U] + c, gu[:, ds(c * PAIR + D_FF, PAIR)], first=layer == 0 and isinstance(c, int) and c == 0)
                    load_down(use[W2] + c, down[ds(c * PAIR, PAIR), :])
                return chunk

            rows = sg[:, 0, 0:P]
            srcs = [norm_mix_pre[0], norm_mix_pre[1], norm_ffn_pre[0], norm_ffn_pre[1], kv_norm, a_b_in[0]]
            at = 0
            for src in srcs:
                r = src.rearrange("(k p) -> k p", p=P)
                sp.dma_start(rows[at:at + r.shape[0], :], r).then_inc(consts, 16)
                at += r.shape[0]
            norm_loads(0)
            w_in = a_w_in[0]
            load_in(G, 0, w_in[:, GMLP_FFN - PAIR:GMLP_FFN], first=True)
            for m in range(2):
                norm_tile(0, m, m, True)
            load_in(W2, 0, w_in[:, GMLP_FFN - 2 * PAIR:GMLP_FFN - PAIR], first=True)
            sp.dma_start(gpost[:, :].rearrange("p (g j) -> p g j", g=GROUPS),
                         a_w_s[0].rearrange("g i j -> i g j")).then_inc(ws_loaded, 16)
            for g in range(NKV):
                for t in range(2):
                    sp.dma_start(sink[t * HEAD:(t + 1) * HEAD, g, :],
                                 b_sinks[0:1, g * 8 + t:(g + 1) * 8:2].to_broadcast([HEAD, NPAIR]),
                                 allow_slow_non_contiguous=True).then_inc(sink_loaded, 16)
            norm(0, start=2)
            sp.wait_ge(rt_ready, TT)
            sp.dma_start(bs[:, :, :].rearrange("p g i -> p (g i)"),
                         a_b_s[0:1].rearrange("a g i -> a (g i)").to_broadcast([P, D])).then_inc(bs_loaded, 16)

            def load_ln(g):
                for e, src in enumerate((a_ln_g, a_ln_b)):
                    sp.dma_start(lngb[:, e, :], src[0:1, ds(g * PAIR, PAIR)].to_broadcast([P, PAIR])).then_inc(loaded[U], 16)

            load_ln(0)

            def park_v(p):
                sp.wait_ge(vtr_free, p * 4 + 4)
                sp.dma_start(v_dram[ds(p * -1 + (GMLP_CHUNKS - 2), 1)].rearrange("a p n -> (a p) n"), raw[U][:, :]).then_inc(v_parked, 16)

            with sp.Fori(0, V_TILES // 4 - 1) as i:
                for e, s in enumerate((G, W2)):
                    load_in(s, i + 1, w_in[:, ds(i * (-2 * PAIR) + (GMLP_FFN - (3 + e) * PAIR), PAIR)])
                    park_v(i * 2 + e)
            load_in(G, USE_GMLP[G], w_in[:, 0:PAIR])
            park_v(GMLP_CHUNKS - 2)
            load_down(USE_GMLP[W2], a_w_out[0, 0:PAIR, :])

            def load_v(g):
                sp.dma_start(raw[U][:, :], v_dram[ds(g - 1, 1)].rearrange("a p n -> (a p) n")).then_inc(loaded[U], 16)
                load_ln(g)

            sp.wait_ge(v_parked, 16 * (GMLP_CHUNKS - 1))
            with sp.Fori(1, GMLP_CHUNKS) as g:
                load_in(G, g + USE_GMLP[G], w_in[:, ds(g * PAIR, PAIR)])
                sp.wait_ge(normed_v, g)
                load_v(g)
                load_down(g + USE_GMLP[W2], a_w_out[0, ds(g * PAIR, PAIR), :])

            chunk = ffn(0)
            sp.wait_ge(normed_v, GMLP_CHUNKS)
            chunk(0)
            sp.wait_ge(prod_ready, 2 * 2 * GMLP_CHUNKS)
            norm_loads(1)
            norm(1)
            with sp.Fori(1, FFN_CHUNKS) as c:
                chunk(c)

            def load_q(s, use, j):
                sp.wait_ge(w_ready[s], use)
                for b in range(2):
                    for g in range(NKV):
                        dst = raw[s][:, :].rearrange("p (k b g f) -> p k b g f", k=KT, b=2, g=NKV)[:, :, b, g, :]
                        at = (g * 8 + j * 2 + b) * HEAD
                        src = b_w_q[0][:, at:at + HEAD].rearrange("(k p) f -> p k f", p=P)
                        sp.dma_start(dst, src).then_inc(loaded[s], 16)

            load_in(G, USE_KV[G], w_kv)
            load_q(U, USE_Q[U], 0)
            for par in range(2):
                sp.wait_ge(h_stored[par], 16 * (TT // 2))
            norm_loads(2)

            def more_loads():
                load_q(G, USE_Q[G], 1)
                sp.wait_ge(down_full, DOWN_BANKS * DOWN_O)
                sp.dma_start(cosT[:, :], rope_cos).then_inc(rope_loaded, 16)
                sp.dma_start(sinT[:, :], rope_sin).then_inc(rope_loaded, 16)

            norm(2, more_loads)
            for j in range(2, Q_PAIRS):
                load_q((U, G)[j % 2], (USE_Q[U], USE_Q[G])[j % 2] + j // 2, j)

            def load_o(j):
                s = (W2, U)[j % 2]
                if j:
                    sp.wait_ge(w_ready[s], USE_O[s] + j // 2)
                else:
                    sp.wait_ge(q_done, 2 + 2 * (D // P))
                for g in range(NKV):
                    dst = raw[s][g * HEAD:(g + 1) * HEAD, :].rearrange("p (t n) -> p t n", t=2)
                    lo = g * 512 + j * 2 * HEAD
                    src = b_w_o[0][lo:lo + 2 * HEAD, :].rearrange("(t p) n -> p t n", p=HEAD)
                    sp.dma_start(dst, src).then_inc(loaded[s], 16)

            for j in range(Q_PAIRS):
                load_o(j)
            sp.wait_ge(o_full, NKV * NCHUNK)
            norm_loads(3)
            chunk = ffn(1)
            chunk(0)
            norm(3)
            with sp.Fori(1, FFN_CHUNKS) as c:
                chunk(c)
            for par in range(2):
                sp.wait_ge(h_stored[par], 16 * (TT // 2) * 3)
            norm_loads(4)
            norm(4)
            for par in range(2):
                sp.wait_ge(h_stored[par], 16 * (TT // 2) * 4)

        @block.gpsimd
        def _(pool):
            total = {"gain": 0, "split": 0}

            def body(i, rounds, uses):
                gains, done = KT * sum(u[3] is not None for u in uses), 0
                for n, (s, use, data, gain, free) in enumerate(uses):
                    pool.wait_ge(*data)
                    if gain is not None:
                        pool.nop(nofuse=True)
                        for k in range(KT):
                            r = raw[s][:, k * PAIR:(k + 1) * PAIR]
                            nc.gpsimd.tensor_scalar(r, r, cols[:, gain + k:gain + k + 1], 0.0, ALU.mult, ALU.add).then_inc(gain_step, 1)
                        done += KT
                        pool.wait_ge(gain_step, i * gains + (total["gain"] + done))
                    if free is not None:
                        pool.wait_ge(*free)
                    pool.nop(nofuse=True)
                    nc.gpsimd.tensor_scalar(WH[s][:, :], raw[s][:, :], 1.0, 0.0, ALU.mult, ALU.add).then_inc(split_step, 1)
                    pool.wait_ge(split_step, i * len(uses) + (total["split"] + n + 1))
                    nc.gpsimd.tensor_tensor(WL[s][:, :], raw[s][:, :], f(WH[s][:, :]), ALU.subtract).then_inc(w_ready[s], 1)
                total["gain"] += gains * rounds
                total["split"] += len(uses) * rounds

            nc.gpsimd.memset(ident[:, :], 0.0).then_inc(pool_step, 1)
            pool.wait_ge(pool_step, 1)
            nc.gpsimd.affine_select(out=ident[:, :], in_=ident[:, :], compare_op=ALU.not_equal, fill=1.0,
                                    base=0, pattern=[[-1, P]], channel_multiplier=1).then_inc(ident_done, 1)

            def zero_acc(n):
                for m in range(TT):
                    pool.wait_ge(tr_full, TR_NORM(n) + 2 * m + 2)
                    nc.gpsimd.memset(acc[:, m, :], 0.0).then_inc(acc_zero, 1)

            pool.wait_ge(tr_free, 1)
            gm = GAIN_MIX[0]
            body(0, 1, [(s, 0, (loaded[s], 16), gm, None) for s in (G, W2)])
            zero_acc(0)
            with pool.Fori(0, V_TILES // 4 - 1) as i:
                body(i, V_TILES // 4 - 1, [(s, i + 1, (loaded[s], i * 16 + 32), gm, (proj_full, i * 8 + v))
                                           for s, v in ((G, 4), (W2, 8))])

            def gmlp(g, frees):
                return [(G, g + USE_GMLP[G], (loaded[G], (g + USE_GMLP[G]) * 16 + 16), gm, frees[0]),
                        (W2, g + USE_GMLP[W2], (loaded[W2], (g + USE_GMLP[W2]) * 16 + 16), None, frees[1])]
            body(0, 1, gmlp(0, ((proj_full, 2 * V_TILES - 4), (proj_full, 2 * V_TILES))))
            with pool.Fori(0, GMLP_CHUNKS - 1) as i:
                body(i, GMLP_CHUNKS - 1, gmlp(i + 1, ((act_full, i * 4 + 4),
                                                      (down_full, i * 2 * DOWN_BANKS + 2 * DOWN_BANKS))))

            loads_ffn0 = (USE_FFN0[G], 3 * GMLP_CHUNKS - 1, USE_FFN0[W2])
            loads_kv = tuple(n + FFN_CHUNKS for n in loads_ffn0)
            loads_q = (loads_kv[0] + 1, loads_kv[1], loads_kv[2])
            loads_o = (loads_q[0] + 2 * Q_PAIRS, loads_q[1] + 2 * Q_PAIRS, loads_q[2])
            loads_ffn1 = (loads_o[0], loads_o[1] + Q_PAIRS, loads_o[2] + Q_PAIRS)

            def ffn(layer, n, before):
                use, loads = ((USE_FFN0, loads_ffn0), (USE_FFN1, loads_ffn1))[layer]
                st, dn, gain = STAGE_FFN[layer], (DOWN_FFN0, DOWN_FFN1)[layer], GAIN_FFN[layer]

                def uses(c, frees):
                    return [(s, c + use[s], (loaded[s], c * 16 + 16 * (loads[s] + 1)), g, frees[s])
                            for s, g in ((G, gain), (U, gain), (W2, None))]
                body(0, 1, uses(0, before))
                zero_acc(n)
                with pool.Fori(0, FFN_CHUNKS - 1) as i:
                    body(i, FFN_CHUNKS - 1, uses(i + 1, ((act_full, i * 4 + (2 * st + 4)), (mul_full, i * 4 + (2 * st + 4)),
                                                         (down_full, i * 2 * DOWN_BANKS + (dn + 2) * DOWN_BANKS))))

            ffn(0, 1, ((act_full, 2 * STAGE_FFN[0]), (mul_full, 2 * STAGE_FFN[0]), (down_full, DOWN_BANKS * DOWN_FFN0)))
            end_ffn0 = 2 * STAGE_FFN[1]
            body(0, 1, [(G, USE_KV[G], (loaded[G], 16 * (loads_kv[G] + 1)), GAIN_KV, (act_full, end_ffn0))])
            for j in range(Q_PAIRS):
                s = (U, G)[j % 2]
                free = (mul_full, end_ffn0) if j == 0 else (proj_full, PROJ_Q + 4 * (j - 1))
                body(0, 1, [(s, USE_Q[s] + j // 2, (loaded[s], 16 * (loads_q[s] + 4 * (j // 2 + 1))), GAIN_MIX[1], free)])

            def stage_q(n, par):
                if not isinstance(n, int) or n > 1:
                    wait_apart(pool, s_full, n * NKV - NKV)
                nc.gpsimd.tensor_copy(qc[par][:, :], qT[:, ds(n * KT * CHUNK, KT * CHUNK)]).then_inc(q_staged, 1)

            def stage_v(n, par, m):
                if not isinstance(n, int) or n > 1:
                    wait_apart(pool, o_full, n * NKV - NKV)
                src = (vshift, vt)[par][:, ds(m, 1), :].rearrange("p a n -> p (a n)")
                nc.gpsimd.tensor_copy(vc[par][:, :], src).then_inc(v_staged, 1)

            pool.wait_ge(q_done, 2 + 2 * (D // P) - 2)
            pool.wait_ge(v_copied, 2)
            pool.wait_ge(proj_full, PROJ_END)
            stage_q(0, 0)
            stage_q(1, 1)
            stage_v(0, 0, 0)
            stage_q(2, 0)
            stage_v(1, 1, 0)
            pool.wait_ge(q_done, 2 + 2 * (D // P))
            with pool.Fori(1, NCHUNK // 2 - 1) as m:
                stage_q(m * 2 + 1, 1)
                stage_v(m * 2, 0, m)
                stage_q(m * 2 + 2, 0)
                stage_v(m * 2 + 1, 1, m)
            stage_q(NCHUNK - 1, 1)
            for n in (NCHUNK - 2, NCHUNK - 1):
                stage_v(n, n % 2, n // 2)

            for j in range(Q_PAIRS):
                s = (W2, U)[j % 2]
                free = (proj_full, PROJ_Q + 12) if j == 1 else (down_full, DOWN_BANKS * (DOWN_O + 2 * max(j - 1, 0)))
                body(0, 1, [(s, USE_O[s] + j // 2, (loaded[s], 16 * (loads_o[s] + 2 * (j // 2 + 1))), None, free)])
            ffn(1, 3, ((o_full, NKV * NCHUNK), (down_full, DOWN_BANKS * DOWN_FFN1), (down_full, DOWN_BANKS * (DOWN_FFN1 - 1))))

        @block.tensor
        def _(pe):
            def pair3(dst, wh, wl, xh, xl, first, last):
                nc.tensor.matmul(dst, wh, xh, start=first, stop=False)
                nc.tensor.matmul(dst, wh, xl, start=False, stop=False)
                return nc.tensor.matmul(dst, wl, xh, start=False, stop=last)

            def project(dst, s, tile, b, half, midway=None):
                wh, wl = tile(WH[s], b), tile(WL[s], b)
                for k in range(KT):
                    if midway is not None and k == KT // 2:
                        midway()
                    t = slice(half * HALF, (half + 1) * HALF)
                    mm = pair3(dst, wh(k), wl(k), XH[:, k, t], XL[:, k, t], k == 0, k == KT - 1)
                return mm

            def down(n, half_of_x=None, x_pair=None, s=W2):
                for m in range(4):
                    for o in range(2):
                        q = m * 2 + o
                        if not (isinstance(n, int) and n * DOWN_BANKS + q < 2):
                            pe.wait_ge(down_added, n * DOWN_BANKS + (q - 1))
                        dst = bank[4 + q % 2][:, :]
                        for t in range(2):
                            if x_pair is None:
                                lh, ll = hidH[:, t, m * P:(m + 1) * P], hidL[:, t, m * P:(m + 1) * P]
                            else:
                                tok = slice(half_of_x * HALF + m * P, half_of_x * HALF + (m + 1) * P)
                                lh, ll = XH[:, x_pair + t, tok], XL[:, x_pair + t, tok]
                            c = slice(t * D + o * HALF, t * D + (o + 1) * HALF)
                            nc.tensor.matmul(dst, lh, WH[s][:, c], start=(t == 0), stop=False)
                            nc.tensor.matmul(dst, lh, WL[s][:, c], start=False, stop=False)
                            mm = nc.tensor.matmul(dst, ll, WH[s][:, c], start=False, stop=(t == 1))
                        mm.then_inc(down_full, 1)

            def transposes(src, dst):
                for q in range(4):
                    mm = nc.tensor.transpose(dst[:, q * P:(q + 1) * P], src[:, q * P:(q + 1) * P], ident[:, :])
                return mm

            def norm_tile(n, m):
                pe.wait_ge(rt_ready, m + (TT * n + 1))
                for q in range(2):
                    before = m * 2 + TR_NORM(n) + q - 1
                    pe.wait_ge(tr_free, max(before, TR_COLS))
                    transposes(acc[:, m, q * HALF:(q + 1) * HALF], bank[6 + q]).then_inc(tr_full, 1)

            def x_ready(n, half):
                pe.wait_ge(tr_free, TR_NORM(n) + TT * (half + 1))

            def stage_ins(stage, half, s, full, first_bank, after=lambda b: None):
                free = act_ready if first_bank == 0 else prod_ready
                for b in range(2):
                    if not (isinstance(stage, int) and stage == 0):
                        pe.wait_ge(free, stage * 2 + (b - 1))
                    project(bank[first_bank + b][:, :], s, in_tile, b, half).then_inc(full, 1)
                    after(b)

            def hidden_ready(stage):
                pe.wait_ge(hid_hi, stage * 2 + 2)
                pe.wait_ge(hid_lo, stage * 2 + 2)

            def mix(stage, group, half):
                wg = wsT[:, ds(group, 1), :].rearrange("p a i -> p (a i)")
                for b in range(2):
                    if not (isinstance(stage, int) and stage == 0):
                        pe.wait_ge(prod_ready, stage * 2 + (b - 1))
                    for q in range(4):
                        m = half * 4 + q
                        dst = bank[2 + b][:, q * P:(q + 1) * P]
                        mm = nc.tensor.matmul(dst, vn[:, m, b * P:(b + 1) * P], wg, start=True, stop=True)
                    mm.then_inc(mul_full, 1)

            def ffn_chunk(layer, c, first):
                use = (USE_FFN0, USE_FFN1)[layer]
                base, dbase = STAGE_FFN[layer], (DOWN_FFN0, DOWN_FFN1)[layer]
                n = 2 * layer + 1
                for h in range(2):
                    st = c * 2 + (base + h)
                    with_norm = first and h == 0
                    if h == 0:
                        pe.wait_ge(w_ready[G], c + (use[G] + 1))
                    stage_ins(st, h, G, act_full, 0, (lambda b: norm_tile(n, 4 + b)) if with_norm else lambda b: None)
                    if not (first and h == 0):
                        down_step(c * 2 + (base + h - 1), c * 2 + (dbase + h - 1), use, c, h)
                    if h == 0:
                        pe.wait_ge(w_ready[U], c + (use[U] + 1))
                    stage_ins(st, h, U, mul_full, 2, (lambda b: norm_tile(n, 6 + b)) if with_norm else lambda b: None)
                    if with_norm:
                        x_ready(n, 1)

            def down_step(stage, n, use, c, h):
                hidden_ready(stage)
                if h == 1:
                    pe.wait_ge(w_ready[W2], c + (use[W2] + 1))
                down(n)

            def gmlp_chunk(g, first):
                for h in range(2):
                    st = g * 2 + h
                    if h == 0:
                        pe.wait_ge(w_ready[G], g + (USE_GMLP[G] + 1))
                    stage_ins(st, h, G, act_full, 0)
                    if not (first and h == 0):
                        down_step(g * 2 + (h - 1), g * 2 + (h - 1), USE_GMLP, g, h)
                    if h == 0:
                        pe.wait_ge(normed_v, g + 1)
                    mix(st, g, h)

            pe.wait_ge(consts, 16 * 6)
            pe.wait_ge(ident_done, 1)
            nc.tensor.transpose(bank[6][:, 0:NCOLS], sg[0:NCOLS, 0, 0:P], ident[0:NCOLS, 0:NCOLS]).then_inc(tr_full, 1)
            for m in range(TT // 2):
                norm_tile(0, m)
            x_ready(0, 0)

            def w_s_back():
                pe.wait_ge(ws_masked, 1)
                for q in range(2):
                    pe.wait_ge(tr_free, TR_WS + q - 1)
                    transposes(gpost[:, q * HALF:(q + 1) * HALF], bank[6 + q]).then_inc(tr_full, 1)
                pe.wait_ge(tr_free, TR_WS + 2)

            def v_back(idx, par):
                pe.wait_ge(v_act, idx + 1)
                if not (isinstance(idx, int) and idx < 2):
                    pe.wait_ge(vtr_free, idx - 1)
                transposes(sg[:, par, :], bank[6 + par]).then_inc(vtr_full, 1)

            def v_pair(i, s, e, first):
                pe.wait_ge(w_ready[s], i + 1)
                for h in range(2):
                    for b in range(2):
                        q = 4 * e + 2 * h + b
                        idx = i * 8 + q
                        if not (first and q < 4):
                            pe.wait_ge(v_act, idx - 3)
                        early = first and q < 2
                        if first and q == 2:
                            x_ready(0, 1)
                        project(bank[(2 * h + b)][:, :], s, in_tile, b, h,
                                midway=(lambda: norm_tile(0, 4 + 2 * q)) if early else None).then_inc(proj_full, 1)
                        if early:
                            norm_tile(0, 5 + 2 * q)
                        else:
                            if first and q == 2:
                                w_s_back()
                                v_back(0, 0)
                            v_back(idx - 1, (q - 1) % 2)

            for e, s in enumerate((G, W2)):
                v_pair(0, s, e, True)
            with pe.Fori(1, V_TILES // 4) as i:
                for e, s in enumerate((G, W2)):
                    v_pair(i, s, e, False)
            v_back(2 * V_TILES - 1, 1)

            pe.wait_ge(v_act, 2 * V_TILES)
            gmlp_chunk(0, True)
            with pe.Fori(1, GMLP_CHUNKS) as g:
                gmlp_chunk(g, False)

            def ffn(layer, n):
                ffn_chunk(layer, 0, True)
                with pe.Fori(1, FFN_CHUNKS) as c:
                    ffn_chunk(layer, c, False)

            def last_down(stage, n, norm):
                if norm == 2:
                    norm_tile(norm, 0)
                hidden_ready(stage)
                down(n)
                if norm < 4:
                    for m in range(1 if norm == 2 else 0, TT // 2):
                        norm_tile(norm, m)
                    x_ready(norm, 0)

            last_down(STAGE_FFN[0] - 1, DOWN_FFN0 - 1, 1)
            ffn(0, 1)
            last_down(STAGE_FFN[1] - 1, DOWN_O - 1, 2)
            pe.wait_ge(w_ready[G], USE_KV[G] + 1)
            for h in range(2):
                if h:
                    x_ready(2, 1)
                for b in range(2):
                    project(bank[2 * b + h][:, :], G, in_tile, b, h,
                            midway=None if h else lambda: norm_tile(2, 4 + 2 * b)).then_inc(proj_full, 1)
                    if h == 0:
                        norm_tile(2, 5 + 2 * b)
            for j in range(Q_PAIRS):
                s = (U, G)[j % 2]
                pe.wait_ge(w_ready[s], USE_Q[s] + j // 2 + 1)
                for h in range(2):
                    for b in range(2):
                        q = 4 * j + 2 * h + b
                        if q in (2, 3):
                            pe.wait_ge(vT_copied, q - 1)
                        else:
                            pe.wait_ge(q_copied, q + 1 if q < 2 else q - 1)
                        project(bank[2 * h + b][:, :], s, in_tile, b, h).then_inc(proj_full, 1)
                        if q == 1:
                            for half in range(2):
                                pe.wait_ge(vT_copied, half + 1)
                                transposes(sg[:, half, :], bank[6 + half]).then_inc(vtr_full, 1)

            def scores(n, par, kv):
                u = n * NKV + kv
                first = isinstance(n, int) and n == 0
                if not first:
                    pe.wait_ge(s_exp, u - 1)
                lo = CHUNK if first else 0
                keys = slice(0, CHUNK) if first else ds(n * CHUNK - CHUNK, P)
                if kv == 0:
                    pe.wait_ge(q_staged, n + 1)
                for j in range(NPAIR):
                    mm = nc.tensor.matmul(bank[kv][:, j * P + lo:(j + 1) * P], qc[par][:, j * P:(j + 1) * P],
                                          kz[kv][:, keys], start=True, stop=True)
                mm.then_inc(s_full, 1)

            def probs_back(n, kv):
                u = n * NKV + kv
                pe.wait_ge(s_norm, u * 3 + 3)
                if not (isinstance(n, int) and n == 0):
                    pe.wait_ge(p_copied, u - 1)
                for j in range(NPAIR):
                    mm = nc.tensor.transpose(bank[6 + kv][:, j * P:(j + 1) * P], prob[kv][:, j, :], ident[:, :])
                mm.then_inc(p_full, 1)

            def values(n, par, kv):
                u = n * NKV + kv
                pe.wait_ge(p_copied, u + 1)
                if not (isinstance(n, int) and n == 0):
                    pe.wait_ge(o_lo, u - 1)
                pe.wait_ge(v_staged, n + 1)
                nc.tensor.matmul(bank[2 + kv][:, :], vc[par][:, :], pT[kv][:, :], start=True, stop=True).then_inc(o_full, 1)

            def attend(n, par):
                known = isinstance(n, int)
                for kv in range(NKV):
                    if not known or n < NCHUNK:
                        scores(n, par, kv)
                    if not known or n >= 2:
                        values(n - 2, par, kv)
                    if not known or 1 <= n <= NCHUNK:
                        probs_back(n - 1, kv)

            for n in range(4):
                attend(n, n % 2)
            with pe.Fori(2, NCHUNK // 2) as m:
                attend(m * 2, 0)
                attend(m * 2 + 1, 1)
            attend(NCHUNK, 0)
            attend(NCHUNK + 1, 1)

            pe.wait_ge(o_lo, NKV * NCHUNK)
            for i, (j, h) in enumerate(O_ORDER):
                s = (W2, U)[j % 2]
                if h == 0:
                    pe.wait_ge(w_ready[s], USE_O[s] + j // 2 + 1)
                down(DOWN_O + i, half_of_x=h, x_pair=2 * j, s=s)
                if i == len(O_ORDER) - 2:
                    norm_tile(3, 0)
            for m in (1, 2, 3):
                norm_tile(3, m)
            x_ready(3, 0)
            ffn(1, 3)
            last_down(STAGES - 1, DOWN_END - 1, 4)

        @block.scalar
        def _(act):
            def norm_step(n, k, par, has1, has2, has3):
                post, pre = n > 0, n < 4
                base_step = STEP_BASE[n]
                one, two = has1 and post, has2 and pre
                if one or two:
                    if not (isinstance(k, int) and k + base_step <= 0):
                        wait_apart(act, ms_done, k + base_step)
                if one:
                    op = nc.scalar.activation(junk[:, :], acc[:, ds(k, 1), :].rearrange("p a n -> p (a n)"),
                                              ACT.Square, accum_out=ssq[:, 0:1])
                if two:
                    other = 1 - par
                    if post:
                        wait_apart(act, h_new, k + TT * (n - 1))
                        src = hout[:, other, :]
                    else:
                        wait_apart(act, h_loaded[other], (k - 1 - other) * 8 + 16)
                        src = hin[:, other, :]
                    op = nc.scalar.activation(acc[:, ds(k - 1, 1), :].rearrange("p a n -> p (a n)"), src,
                                              ACT.Square, accum_out=ssq[:, 1:2])
                if one or two:
                    op.then_inc(sq_done, 1)
                    c = slice(0 if one else 1, 2 if two else 1)
                    act.wait_ge(ms_done, k + (base_step + 1))
                    nc.scalar.activation(root[:, c], rms[:, c], ACT.Sqrt).then_inc(root_done, 1)
                if has3 and pre:
                    m = k - 2
                    for q in range(2):
                        wait_apart(act, tr_full, m * 2 + (TR_NORM(n) + q + 1))
                        nc.scalar.activation(XH[:, 4 * q:4 * q + 4, ds(m * P, P)],
                                             bank[6 + q][:, :].rearrange("p (k t) -> p k t", k=4),
                                             ACT.Copy).then_inc(tr_hi, 1)

            def first_steps(n, steps):
                for k in steps:
                    norm_step(n, k, k % 2, True, k > 0, k > 1)

            def last_steps(n):
                if n:
                    act.wait_ge(down_added, DOWN_BANKS * DOWN_BEFORE_NORM[n])
                with act.Fori(TT // 4, TT // 2) as j:
                    norm_step(n, j * 2, 0, True, True, True)
                    norm_step(n, j * 2 + 1, 1, True, True, True)
                if n < 4:
                    norm_step(n, TT, 0, False, True, True)
                    norm_step(n, TT + 1, 1, False, False, True)

            first_steps(0, range(4))
            last_steps(0)

            def v_gelu(i, q, first):
                idx = i * 8 + q
                act.wait_ge(proj_full, idx + 1)
                if not (first and q < 2):
                    act.wait_ge(vtr_full, idx - 1)
                act.nop(nofuse=True)
                nc.scalar.activation(sg[:, q % 2, :], bank[q % 4][:, :], ACT.Gelu_apprx_tanh,
                                     bias=cols[:, ds(i * -4 + (BIAS_IN + 2 * V_TILES - 2 - 2 * (q // 4) + q % 2), 1)]).then_inc(v_act, 1)

            for q in range(8):
                v_gelu(0, q, True)
            with act.Fori(1, V_TILES // 4) as i:
                for q in range(8):
                    v_gelu(i, q, False)
            act.wait_ge(v_stat, 2)
            nc.scalar.activation(vrstd[:, :], vrstd[:, :], ACT.Sqrt).then_inc(v_root, 1)

            def stage(st, func, bias, first=False, between=lambda: None):
                for b in range(2):
                    act.wait_ge(act_full, st * 2 + (b + 1))
                    if not first:
                        act.wait_ge(hid_lo, st * 2 + (b - 1))
                    act.nop(nofuse=True)
                    if bias is None:
                        nc.scalar.activation(sg[:, b, :], bank[b][:, :], func).then_inc(act_ready, 1)
                    else:
                        nc.scalar.activation(sg[:, b, :], bank[b][:, :], func, bias=bias(b)).then_inc(act_ready, 1)

                between()
                for b in range(2):
                    act.wait_ge(prod_ready, st * 2 + (b + 1))
                    nc.scalar.activation(hidH[:, b, :], sg[:, b, :], ACT.Copy).then_inc(hid_hi, 1)

            def gmlp(g, first):
                for h in range(2):
                    stage(g * 2 + h, ACT.Gelu_apprx_tanh, lambda b: cols[:, ds(g * 2 + (BIAS_IN + b), 1)], first and h == 0)

            act.wait_ge(vtr_full, 2 * V_TILES)
            gmlp(0, True)
            with act.Fori(1, GMLP_CHUNKS) as g:
                gmlp(g, False)

            def early_steps(n):
                act.wait_ge(down_added, DOWN_BANKS * (DOWN_BEFORE_NORM[n] - 1))
                first_steps(n, (0, 1))

            def ffn(layer):
                n = 2 * layer + 2
                with act.Fori(0, 2 * FFN_CHUNKS - 1) as c:
                    stage(c + STAGE_FFN[layer], ACT.Silu, None)
                stage(STAGE_FFN[layer] + 2 * FFN_CHUNKS - 1, ACT.Silu, None, between=lambda: early_steps(n))
                first_steps(n, (2, 3))
                last_steps(n)

            early_steps(1)
            first_steps(1, (2, 3))
            last_steps(1)
            ffn(0)

            def plain_and_rotated(r, full, src):
                e = r % 2
                act.wait_ge(proj_full, full)
                if r >= 2:
                    act.wait_ge(q_done, r - 1)
                nc.scalar.activation(qplain[e], src[:, :], ACT.Copy)
                for q in range(4):
                    a, b = q * 32, (q ^ 1) * 32
                    op = nc.scalar.activation(qrot[e][a:a + 32, :], src[b:b + 32, :], ACT.Copy)
                op.then_inc(q_copied, 1)

            for h in range(2):
                plain_and_rotated(h, PROJ_KV + 2 * h + 1, bank[h])
                act.wait_ge(proj_full, PROJ_KV + 2 * h + 2)
                nc.scalar.activation(sg[:, h, :], bank[2 + h][:, :], ACT.Copy).then_inc(vT_copied, 1)
            plain_and_rotated(2, PROJ_Q + 1, bank[0])
            for h in range(2):
                act.wait_ge(vtr_full, 2 * V_TILES + h + 1)
                src = bank[6 + h][:, :].rearrange("p (m d) -> p m d", m=4)
                after = min(4, TT - 1 - 4 * h)
                nc.scalar.activation(vshift[CHUNK:P, 4 * h:4 * h + 4, :], src[0:CHUNK], ACT.Copy)
                nc.scalar.activation(vshift[0:CHUNK, 4 * h + 1:4 * h + 1 + after, :], src[CHUNK:P, 0:after, :], ACT.Copy)
                nc.scalar.activation(vt[:, 4 * h:4 * h + 4, :], src, ACT.Copy).then_inc(v_copied, 1)
            for q in range(1, 2 * (D // P)):
                plain_and_rotated(2 + q, PROJ_Q + q + 1, bank[q % 4])

            def exps(n, kv):
                u = n * NKV + kv
                first = isinstance(n, int) and n == 0
                act.wait_ge(s_max, u * 3 + 3)
                if not first:
                    act.wait_ge(p_full, u - 1)
                lo = CHUNK if first else 0
                nc.scalar.activation(a_snk[:, kv, :], a_off[:, kv, :], ACT.Exp)
                for j in range(NPAIR):
                    op = nc.scalar.activation(prob[kv][:, j, lo:P], bank[kv][:, j * P + lo:(j + 1) * P], ACT.Exp,
                                              bias=a_neg[:, kv, j:j + 1], scale=SCALE, accum_out=a_sum[:, kv, j:j + 1])
                op.then_inc(s_exp, 1)

            def p_copy(n, kv):
                u = n * NKV + kv
                act.wait_ge(p_full, u + 1)
                if not (isinstance(n, int) and n == 0):
                    act.wait_ge(o_full, u - 1)
                nc.scalar.activation(pT[kv][:, :], bank[6 + kv][:, :], ACT.Copy).then_inc(p_copied, 1)

            def o_split(n, kv):
                u = n * NKV + kv
                wait_apart(act, o_full, u + 1)
                r = slice(kv * HEAD, (kv + 1) * HEAD)
                nc.scalar.activation(XH[r, :, ds(n * CHUNK, CHUNK)],
                                     bank[2 + kv][r, :].rearrange("p (t c) -> p t c", t=KT), ACT.Copy).then_inc(o_hi, 1)

            def attend(n):
                known = isinstance(n, int)
                for kv in range(NKV):
                    if not known or 1 <= n <= NCHUNK:
                        p_copy(n - 1, kv)
                    if not known or n < NCHUNK:
                        exps(n, kv)
                    before = n - 2 + kv
                    if not known or 0 <= before < NCHUNK:
                        o_split(before, 1 - kv)

            attend(0)
            attend(1)
            with act.Fori(2, NCHUNK) as n:
                attend(n)
            attend(NCHUNK)
            attend(NCHUNK + 1)
            act.wait_ge(down_added, DOWN_BANKS * (DOWN_BEFORE_NORM[3] - 2))
            first_steps(3, range(4))
            last_steps(3)
            ffn(1)

        @block.vector
        def _(dve):
            def add_piece(n, q, half, copy=False):
                m, o = q // 2, q % 2
                dve.wait_ge(down_full, n * DOWN_BANKS + (q + 1))
                a = acc[:, 4 * half + m, o * HALF:(o + 1) * HALF]
                if copy:
                    nc.vector.tensor_copy(a, bank[4 + q % 2][:, :]).then_inc(down_added, 1)
                else:
                    nc.vector.tensor_tensor(a, bank[4 + q % 2][:, :], a, ALU.add).then_inc(down_added, 1)

            def add_down(n, copy=False, half=0):
                for q in range(DOWN_BANKS):
                    add_piece(n, q, half, copy)

            def norm_step(n, k, par, has1, has2, has3, down=None):
                post, pre = n > 0, n < 4
                base_step = STEP_BASE[n]
                one, two = has1 and post, has2 and pre

                def piece(i):
                    if down is not None and i < len(down[1]):
                        add_piece(down[0], down[1][i], 1)

                if one or two:
                    c = slice(0 if one else 1, 2 if two else 1)
                    dve.wait_ge(sq_done, k + (base_step + 1))
                    nc.vector.tensor_scalar(rms[:, c], ssq[:, c], 1.0 / D, EPS, ALU.mult, ALU.add).then_inc(ms_done, 1)
                    piece(0)
                    dve.wait_ge(root_done, k + (base_step + 1))
                    nc.vector.reciprocal(rstd[:, c], root[:, c]).then_inc(rstd_done, 1)
                    dve.wait_ge(rstd_done, k + (base_step + 1))
                if one:
                    if isinstance(k, int) and k == 0:
                        dve.wait_ge(g_loaded, 16 * n)
                    a = acc[:, ds(k, 1), :].rearrange("p a n -> p (a n)")
                    nc.vector.scalar_tensor_tensor(out=a, in0=a, scalar=rstd[:, 0:1], in1=gpost[:, :],
                                                   op0=ALU.mult, op1=ALU.mult).then_inc(scaled, 1)
                    piece(1)
                    dve.wait_ge(h_loaded[par], H_LOADS[n] + (k - par) * 8 + 16)
                    if n > 1 or not isinstance(k, int) or k > 1:
                        dve.wait_ge(h_stored[par], (k - par) * 8 + 16 * (TT // 2) * (n - 1))
                    dve.wait_ge(scaled, k + (TT * (n - 1) + 1))
                    nc.vector.tensor_tensor(hout[:, par, :], hin[:, par, :], a, ALU.add).then_inc(h_new, 1)
                    piece(2)
                if two:
                    src = (hout if post else hin)[:, 1 - par, :]
                    nc.vector.tensor_scalar(acc[:, ds(k - 1, 1), :].rearrange("p a n -> p (a n)"), src,
                                            rstd[:, 1:2], None, ALU.mult).then_inc(rt_ready, 1)
                piece(3)
                if has3 and pre:
                    m = k - 2
                    for q in range(2):
                        dve.wait_ge(tr_hi, m * 2 + (2 * TT * n + q + 1))
                        nc.vector.tensor_tensor(XL[:, 4 * q:4 * q + 4, ds(m * P, P)],
                                                bank[6 + q][:, :].rearrange("p (k t) -> p k t", k=4),
                                                f(XH[:, 4 * q:4 * q + 4, ds(m * P, P)]), ALU.subtract).then_inc(tr_free, 1)
                        piece(4 + q)

            def first_step(n, k, down=None):
                norm_step(n, k, k % 2, True, k > 0, k > 1, down)

            def last_steps(n):
                with dve.Fori(TT // 4, TT // 2) as j:
                    norm_step(n, j * 2, 0, True, True, True)
                    norm_step(n, j * 2 + 1, 1, True, True, True)
                if n < 4:
                    norm_step(n, TT, 0, False, True, True)
                    norm_step(n, TT + 1, 1, False, False, True)

            dve.wait_ge(tr_full, 1)
            nc.vector.tensor_copy(cols[:, :], bank[6][:, 0:NCOLS]).then_inc(tr_free, 1)
            for k in range(4):
                first_step(0, k)
            last_steps(0)
            dve.wait_ge(ws_loaded, 16)
            nc.vector.memset(gpost[0:CHUNK, :].rearrange("p (g j) -> p g j", g=GROUPS)[:, :, CHUNK:P], 0.0).then_inc(ws_masked, 1)
            for q in range(2):
                dve.wait_ge(tr_full, TR_WS + q + 1)
                nc.vector.tensor_copy(wsT[:, 4 * q:4 * q + 4, :], bank[6 + q][:, :].rearrange("p (g i) -> p g i", g=4)).then_inc(tr_free, 1)

            vg = raw[U][:, :].rearrange("p (m d) -> p m d", m=TT)

            def v_copy(i, q, first):
                idx = i * 8 + q
                dve.wait_ge(vtr_full, idx + 1)
                h, b = (q // 2) % 2, q % 2
                if q % 4 == 0 and not (first and q == 0):
                    dve.wait_ge(v_parked, i * 32 + 4 * q)
                src = bank[6 + q % 2][:, :].rearrange("p (m d) -> p m d", m=4)
                for m in range(4):
                    nc.vector.bn_stats(stats[:, 4 * h + m, ds(i * 4 + 2 * (q // 4) + b, 1), :].rearrange("p a s -> p (a s)"), src[:, m, :])
                nc.vector.tensor_copy(vg[:, 4 * h:4 * h + 4, b * P:(b + 1) * P], src).then_inc(vtr_free, 1)

            for q in range(8):
                v_copy(0, q, True)
            with dve.Fori(1, V_TILES // 4) as i:
                for q in range(8):
                    v_copy(i, q, False)
            dve.wait_ge(vtr_free, 2 * V_TILES)
            for m in range(TT):
                op = nc.vector.bn_aggr(vmean[:, m, :], stats[:, m, :, :].rearrange("p a s -> p (a s)"))
            op.then_inc(v_stat, 1)
            dve.wait_ge(v_stat, 1)
            nc.vector.tensor_scalar(vrstd[:, :], vmean[:, :, 1], EPS, None, ALU.add).then_inc(v_stat, 1)
            dve.wait_ge(v_root, 1)
            nc.vector.reciprocal(vrstd[:, :], vrstd[:, :]).then_inc(v_stat, 1)
            dve.wait_ge(v_stat, 3)

            def layer_norm(g):
                dve.wait_ge(loaded[U], g * 48 + 32)
                for m in range(TT):
                    op = nc.vector.tensor_scalar(vg[:, m, :], vg[:, m, :], vmean[:, m, 0:1], vrstd[:, m:m + 1],
                                                 ALU.subtract, ALU.mult)
                op.then_inc(ln_step, 1)
                dve.wait_ge(ln_step, g * 2 + 1)
                lg = lambda e: lngb[:, e:e + 1, :].to_broadcast([P, TT, PAIR])
                nc.vector.tensor_tensor(vg, vg, lg(0), ALU.mult).then_inc(ln_step, 1)
                dve.wait_ge(ln_step, g * 2 + 2)
                if not isinstance(g, int):
                    dve.wait_ge(mul_full, g * 4)
                nc.vector.tensor_tensor(vn[:, :, :], vg, lg(1), ALU.add).then_inc(normed_v, 1)

            def hidden_lo(st, b):
                dve.wait_ge(hid_hi, st * 2 + (b + 1))
                nc.vector.tensor_tensor(hidL[:, b, :], sg[:, b, :], f(hidH[:, b, :]), ALU.subtract).then_inc(hid_lo, 1)

            def gmlp(g, first):
                for h in range(2):
                    st = g * 2 + h
                    if not (first and h == 0):
                        add_down(g * 2 + (h - 1), half=1 - h)
                    for b in range(2):
                        dve.wait_ge(mul_full, st * 2 + (b + 1))
                        mixed = bank[2 + b][:, :].rearrange("p (m i) -> p m i", m=4)
                        nc.vector.tensor_tensor(mixed, mixed, bs[:, ds(g, 1), :].to_broadcast([P, 4, P]), ALU.add).then_inc(bias_done, 1)
                        dve.wait_ge(bias_done, st * 2 + (b + 1))
                        dve.wait_ge(act_ready, st * 2 + (b + 1))
                        nc.vector.tensor_tensor(sg[:, b, :], bank[2 + b][:, :], sg[:, b, :], ALU.mult).then_inc(prod_ready, 1)
                    for b in range(2):
                        hidden_lo(st, b)

            layer_norm(0)
            dve.wait_ge(bs_loaded, 16)
            dve.wait_ge(acc_zero, TT)
            gmlp(0, True)
            with dve.Fori(1, GMLP_CHUNKS) as g:
                layer_norm(g)
                gmlp(g, False)
            for k in range(4):
                first_step(1, k, (DOWN_FFN0 - 1, range(4 * k, 4 * k + 4)) if k < 2 else None)
            last_steps(1)

            def ffn(layer, zeroed):
                base, dbase = STAGE_FFN[layer], (DOWN_FFN0, DOWN_FFN1)[layer]
                dve.wait_ge(acc_zero, zeroed)

                def chunk(c, first, last=False):
                    for h in range(2):
                        st = c * 2 + (base + h)
                        if not (first and h == 0):
                            add_down(c * 2 + (dbase + h - 1), half=1 - h)
                        if last and h == 1:
                            for k in range(2):
                                first_step(n, k)
                        for b in range(2):
                            dve.wait_ge(mul_full, st * 2 + (b + 1))
                            dve.wait_ge(act_ready, st * 2 + (b + 1))
                            nc.vector.tensor_tensor(sg[:, b, :], bank[2 + b][:, :], sg[:, b, :], ALU.mult).then_inc(prod_ready, 1)
                        for b in range(2):
                            hidden_lo(st, b)

                n = 2 * layer + 2
                chunk(0, True)
                with dve.Fori(1, FFN_CHUNKS - 1) as c:
                    chunk(c, False)
                chunk(FFN_CHUNKS - 1, False, last=True)
                split = 5 if n < 4 else 4
                first_step(n, 2, (dbase + 2 * FFN_CHUNKS - 1, range(split)))
                first_step(n, 3, (dbase + 2 * FFN_CHUNKS - 1, range(split, DOWN_BANKS)))
                last_steps(n)

            ffn(0, 2 * TT)

            def rotate(r, e, dsts, half):
                t = slice(half * HALF, (half + 1) * HALF)
                dve.wait_ge(q_copied, r + 1)
                nc.vector.tensor_tensor(qplain[e], qplain[e], cosT[:, t], ALU.mult)
                nc.vector.tensor_tensor(qrot[e], qrot[e], sinT[:, t], ALU.mult).then_inc(rope_step, 1)
                dve.wait_ge(rope_step, r + 1)
                for rows, dst in dsts:
                    by_chunk = lambda a: a[rows, :].rearrange("p (n c) -> p n c", c=CHUNK)
                    op = nc.vector.tensor_tensor(dst, by_chunk(qplain[e]), by_chunk(qrot[e]), ALU.add)
                op.then_inc(q_done, 1)

            nc.vector.memset(vshift[0:CHUNK, 0, :], 0.0)
            for g in range(NKV):
                nc.vector.memset(kz[g][(1 - g) * HEAD:(2 - g) * HEAD, :], 0.0)
            dve.wait_ge(rope_loaded, 32)
            for h in range(2):
                rows = [slice(g * HEAD, (g + 1) * HEAD) for g in range(NKV)]
                rotate(h, h, [(rows[g], kz[g][rows[g], h * HALF:(h + 1) * HALF].rearrange("p (n c) -> p n c", c=CHUNK))
                              for g in range(NKV)], h)
            q_by_chunk = qT.rearrange("p (n t c) -> p n t c", n=NCHUNK, t=KT)
            for q in range(2 * (D // P)):
                h, tile = (q // 2) % 2, 2 * (q // 4) + q % 2
                rotate(2 + q, q % 2, [(slice(0, P), q_by_chunk[:, h * NCHUNK // 2:(h + 1) * NCHUNK // 2, tile, :])], h)

            def maxima(n, kv):
                u = n * NKV + kv
                lo = CHUNK if isinstance(n, int) and n == 0 else 0
                dve.wait_ge(s_full, u + 1)
                sc = bank[kv][:, :].rearrange("p (j m) -> p j m", j=NPAIR)[:, :, lo:P]
                nc.vector.reduce_max(a_max[:, kv, :], sc, AX_X).then_inc(s_max, 1)
                dve.wait_ge(s_max, u * 3 + 1)
                nc.vector.scalar_tensor_tensor(out=a_neg[:, kv, :], in0=a_max[:, kv, :], scalar=-SCALE, in1=neg_sink[:, kv, :],
                                               op0=ALU.mult, op1=ALU.min).then_inc(s_max, 1)
                dve.wait_ge(s_max, u * 3 + 2)
                nc.vector.tensor_tensor(a_off[:, kv, :], sink[:, kv, :], a_neg[:, kv, :], ALU.add).then_inc(s_max, 1)

            def normalise(n, kv):
                u = n * NKV + kv
                dve.wait_ge(s_exp, u + 1)
                nc.vector.tensor_tensor(a_den[:, kv, :], a_sum[:, kv, :], a_snk[:, kv, :], ALU.add).then_inc(s_norm, 1)
                dve.wait_ge(s_norm, u * 3 + 1)
                nc.vector.reciprocal(a_inv[:, kv, :], a_den[:, kv, :]).then_inc(s_norm, 1)
                dve.wait_ge(s_norm, u * 3 + 2)
                inv = a_inv[:, kv, :].unsqueeze(2).to_broadcast([P, NPAIR, P])
                nc.vector.tensor_tensor(prob[kv][:, :, :], prob[kv][:, :, :], inv, ALU.mult).then_inc(s_norm, 1)

            def o_rest(n, kv):
                dve.wait_ge(o_hi, n * NKV + (kv + 1))
                r = slice(kv * HEAD, (kv + 1) * HEAD)
                nc.vector.tensor_tensor(XL[r, :, ds(n * CHUNK, CHUNK)], bank[2 + kv][r, :].rearrange("p (t c) -> p t c", t=KT),
                                        f(XH[r, :, ds(n * CHUNK, CHUNK)]), ALU.subtract).then_inc(o_lo, 1)

            def attend(n):
                known = isinstance(n, int)
                for kv in range(NKV):
                    if not known or n < NCHUNK:
                        maxima(n, kv)
                    before = n - 1 + kv
                    if not known or 0 <= before < NCHUNK:
                        normalise(before, 1 - kv)
                    if not known or n >= 2:
                        o_rest(n - 2, kv)

            dve.wait_ge(sink_loaded, 16 * 4)
            nc.vector.tensor_scalar(neg_sink[:, :, :], sink[:, :, :], -1.0, None, ALU.mult)
            for kv in range(NKV):
                nc.vector.memset(prob[kv][:, :, 0:CHUNK], 0.0)
            attend(0)
            attend(1)
            with dve.Fori(2, NCHUNK) as n:
                attend(n)
            attend(NCHUNK)
            attend(NCHUNK + 1)

            for i, (j, h) in enumerate(O_ORDER[:-2]):
                add_down(DOWN_O + i, copy=(j == 0), half=h)
            for k in range(4):
                first_step(3, k, (DOWN_FFN1 - 2 + k // 2, range(4 * (k % 2), 4 * (k % 2) + 4)))
            last_steps(3)
            ffn(1, 3 * TT)


DOWN_BEFORE_NORM = (0, DOWN_FFN0, DOWN_O, DOWN_FFN1, DOWN_END)
STEPS = [TT, TT + 1, TT + 1, TT + 1, TT]
STEP_BASE = [sum(STEPS[:n]) for n in range(5)]
STEP_BASE[0] = -1
H_LOADS = [16 * (TT // 2) * n for n in range(5)]


def rope_tables():
    pos = np.arange(S, dtype=np.float32)
    inv = (np.float32(1.0) / (np.float32(10000.0) ** (np.arange(0, HEAD, 2, dtype=np.float32) / np.float32(HEAD)))).astype(np.float32)
    ang = (inv[:, None] * pos[None, :]).astype(np.float32)
    c, s = np.cos(ang).astype(np.float32), np.sin(ang).astype(np.float32)
    return np.concatenate([c] * 4, 0), np.concatenate([-s, s, -s, s], 0)


_INS = ["x", "norm_mix_pre", "norm_mix_post", "norm_ffn_pre", "norm_ffn_post", "a_w_in", "a_b_in", "a_ln_g", "a_ln_b",
        "a_w_s", "a_b_s", "a_w_out", "kv_norm", "w_kv", "b_w_q", "b_sinks", "b_w_o", "f_w_gate_up", "f_w_down"]


def kernel(**inputs):
    import concourse.bacc as bacc
    from concourse.bass_utils import run_bass_kernel_spmd

    nc = bacc.Bacc("TRN2", target_bir_lowering=False, num_devices=1)
    cos, sin = rope_tables()
    arrays, args = {}, []
    for name in _INS + ["rope_cos", "rope_sin"]:
        a = cos if name == "rope_cos" else sin if name == "rope_sin" else np.ascontiguousarray(inputs[name])
        arrays[f"in_{name}"] = a
        args.append(nc.dram_tensor(f"in_{name}", a.shape, mybir.dt.from_np(a.dtype), kind="ExternalInput").ap())
    y = nc.dram_tensor("out_y", [1, S, D], F32, kind="ExternalOutput").ap()
    build_trunk(nc, *args, y)
    r = run_bass_kernel_spmd(nc, [arrays], core_ids=[0])
    return r.results[0]["out_y"]
```

```python
import numpy as np

import concourse.bass as bass
from concourse import mybir
from concourse.alu_op_type import AluOpType as ALU

F32 = mybir.dt.float32
F32R = mybir.dt.float32r
ACT = mybir.ActivationFunctionType
AX_X = mybir.AxisListType.X
ds = bass.ds

P = 128
D = 1024
S = 1024
KT = D // P
TT = S // P
HALF = 512
GMLP_FFN = 4 * D
GMLP_HALF = GMLP_FFN // 2
GROUPS = 8
PAIR = 2 * P
assert GMLP_HALF // GROUPS == PAIR
D_FF = -(-8 * D // (3 * 256)) * 256
HEAD = 64
CHUNK = 64
NCHUNK = S // CHUNK
SCALE = 1.0 / float(np.sqrt(HEAD))
EPS = 1e-6
GMLP_CHUNKS = GMLP_HALF // PAIR
FFN_CHUNKS = D_FF // PAIR
Q_PAIRS = D // PAIR
G, U, W2 = 0, 1, 2

GAIN_MIX = (0, 8)
GAIN_FFN = (16, 24)
GAIN_KV = 32
BIAS_IN = 40
NCOLS = BIAS_IN + GMLP_HALF // P

STAGE_FFN = (2 * GMLP_CHUNKS, 2 * GMLP_CHUNKS + 2 * FFN_CHUNKS)
STAGES = STAGE_FFN[1] + 2 * FFN_CHUNKS
DOWN_FFN0 = 2 * GMLP_CHUNKS
DOWN_O = DOWN_FFN0 + 2 * FFN_CHUNKS
DOWN_FFN1 = DOWN_O + 2 * Q_PAIRS
DOWN_END = DOWN_FFN1 + 2 * FFN_CHUNKS
DOWN_BANKS = 8
USE_GMLP = (GROUPS // 2, 0, GROUPS // 2)
USE_FFN0 = (USE_GMLP[0] + GMLP_CHUNKS, 0, USE_GMLP[2] + GMLP_CHUNKS)
USE_KV = tuple(u + FFN_CHUNKS for u in USE_FFN0)
USE_Q = (USE_KV[0] + 1, USE_KV[1], USE_KV[2])
USE_O = (USE_Q[0] + Q_PAIRS // 2, USE_Q[1] + Q_PAIRS // 2, USE_Q[2])
USE_FFN1 = (USE_O[0], USE_O[1] + Q_PAIRS // 2, USE_O[2] + Q_PAIRS // 2)
V_PIECES = 4 * GROUPS
PROJ_KV = V_PIECES
PROJ_Q = PROJ_KV + 4
PROJ_END = PROJ_Q + 2 * (D // P)
TR_COLS = 1
TR_NORM = lambda n: TR_COLS + 2 * TT * n + (2 if n else 0)
TR_WS = TR_COLS + 2 * TT
O_ORDER = ((0, 0), (0, 1), (1, 0), (1, 1), (2, 0), (3, 0), (2, 1), (3, 1))
X_BATCHES = (range(0, 2), range(2, 4), range(4, 8))
NKV = 2
NPAIR = 4


def wait_apart(eng, sem, value):
    eng.wait_ge(sem, value)
    eng.nop(nofuse=True)


def build_trunk(nc, x, norm_mix_pre, norm_mix_post, norm_ffn_pre, norm_ffn_post, a_w_in, a_b_in, a_ln_g,
                a_ln_b, a_w_s, a_b_s, a_w_out, kv_norm, w_kv, b_w_q, b_sinks, b_w_o, f_w_gate_up,
                f_w_down, rope_cos, rope_sin, out):
    KB = 1024
    place = {"at": -(-nc.sbuf_base // 64) * 64}

    def sb(name, shape, dtype=F32, at=None):
        size = int(np.prod(shape[1:])) * 4
        if at is None:
            at = place["at"]
            place["at"] = -(-(at + size) // 64) * 64
        t = nc.alloc_sbuf_tensor_at(name, list(shape), dtype, offset=at)
        return t

    here = lambda: place["at"]

    acc = sb("acc", [P, TT, D])
    XH = sb("XH", [P, KT, S], F32R)
    XL = sb("XL", [P, KT, S], F32R)
    at_w = here()
    WH = [sb(f"WH{s}", [P, 8 * PAIR], F32R) for s in range(3)]
    prob = [sb(f"prob{k}", [P, NPAIR, P], at=at_w + 2 * KB * k) for k in range(NKV)]
    pT = [sb(f"pT{k}", [P, HALF], at=at_w + 4 * KB + 2 * KB * k) for k in range(NKV)]
    qc = [sb(f"qc{e}", [P, KT * CHUNK], at=at_w + 24 * KB + 2 * KB * e) for e in range(2)]
    vc = [[sb(f"vc{e}{k}", [P, P], at=at_w + 28 * KB + (2 * e + k) * KB // 2) for k in range(NKV)] for e in range(2)]
    vn = sb("vn", [P, TT, PAIR], at=at_w + 8 * KB)
    cosT = sb("cosT", [P, S], at=at_w + 16 * KB)
    sinT = sb("sinT", [P, S], at=at_w + 20 * KB)
    WL = [sb(f"WL{s}", [P, 8 * PAIR], F32R) for s in range(3)]
    raw = [sb(f"raw{s}", [P, 8 * PAIR]) for s in range(3)]
    at_hid = here()
    hidH = sb("hidH", [P, 2, HALF], F32R)
    hidL = sb("hidL", [P, 2, HALF], F32R)
    stats = sb("stats", [P, TT, GROUPS, 6], at=at_hid)
    vbias = sb("vbias", [P, 2, PAIR], at=at_hid + 4 * KB)
    vshift = sb("vshift", [P, TT, P], at=at_hid)
    kz1 = sb("kz1", [P, S], at=at_hid + 4 * KB)
    sg = sb("sg", [P, 2, HALF])
    junk = sb("junk", [P, D])
    gpost = sb("gpost", [P, D])
    at_e = here()
    hin = sb("hin", [P, 2, D])
    hout = sb("hout", [P, 2, D])
    wsT = sb("wsT", [P, GROUPS, P], at=at_e)
    bs = sb("bs", [P, GROUPS, P], at=at_e + 8 * KB)
    lngb = sb("lngb", [P, 2, PAIR], at=at_e + 12 * KB)
    kz = [sb("kz0", [P, S], at=at_e), kz1]
    vt = sb("vt", [P, TT, P], at=at_e + 4 * KB)
    ident = sb("ident", [P, P])
    cols = sb("cols", [P, NCOLS])
    sink = sb("sink", [P, NKV, NPAIR])
    vmean = sb("vmean", [P, TT, 2])
    vrstd = sb("vrstd", [P, TT])
    ssq = sb("ssq", [P, 2])
    rms = sb("rms", [P, 2])
    root = sb("root", [P, 2])
    rstd = sb("rstd", [P, 2])
    x_ssq, x_ms, x_root, x_rstd = [sb(name, [P, TT]) for name in ("x_ssq", "x_ms", "x_root", "x_rstd")]
    a_max = sb("a_max", [P, NKV, NPAIR])
    neg_sink = sb("neg_sink", [P, NKV, NPAIR])
    a_neg = sb("a_neg", [P, NKV, NPAIR])
    a_off = sb("a_off", [P, NKV, NPAIR])
    a_snk = sb("a_snk", [P, NKV, NPAIR])
    a_sum = sb("a_sum", [P, NKV, NPAIR])
    a_den = sb("a_den", [P, NKV, NPAIR])
    a_inv = sb("a_inv", [P, NKV, NPAIR])
    qplain = [raw[2][:, e * 1024:e * 1024 + 512] for e in range(2)]
    qrot = [raw[2][:, e * 1024 + 512:(e + 1) * 1024] for e in range(2)]
    qT = acc[:, :, :].rearrange("p m n -> p (m n)")

    x_tile = lambda m: (hin, hout)[m % 4 // 2][:, m % 2, :]

    bank = [nc.alloc_psum_tensor(f"bank{b}", [P, HALF], F32) for b in range(8)]

    h_dram = [nc.dram_tensor(f"h{n}", [TT, P, D], F32, kind="Internal").ap() for n in range(1, 4)]
    v_dram = nc.dram_tensor("v_park", [GMLP_CHUNKS - 1, P, TT * PAIR], F32, kind="Internal").ap()
    x_in = x.rearrange("a (m p) d -> (a m) p d", p=P)
    out_t = out.rearrange("a (m p) d -> (a m) p d", p=P)
    h_from = [x_in, x_in, h_dram[0], h_dram[1], h_dram[2]]
    h_to = [None, h_dram[0], h_dram[1], h_dram[2], out_t]
    post_gain = [None, norm_mix_post[0:1, :], norm_ffn_post[0:1, :], norm_mix_post[1:2, :], norm_ffn_post[1:2, :]]

    sem = nc.alloc_semaphore
    loaded = [sem(f"loaded{s}") for s in range(3)]
    normed_v = sem("normed_v")
    w_ready = [sem(f"w_ready{s}") for s in range(3)]
    pool_step = sem("pool_step")
    proj_full = sem("proj_full")
    act_full = sem("act_full")
    act_ready = sem("act_ready")
    mul_full = sem("mul_full")
    prod_ready = sem("prod_ready")
    hid_hi = sem("hid_hi")
    hid_lo = sem("hid_lo")
    down_full = sem("down_full")
    down_added = sem("down_added")
    acc_zero = sem("acc_zero")
    tr_full = sem("tr_full")
    tr_hi = sem("tr_hi")
    tr_free = sem("tr_free")
    h_loaded = [sem(f"h_loaded{e}") for e in range(2)]
    h_stored = [sem(f"h_stored{e}") for e in range(2)]
    h_new = sem("h_new")
    g_loaded = sem("g_loaded")
    sq_done = sem("sq_done")
    ms_done = sem("ms_done")
    root_done = sem("root_done")
    rstd_done = sem("rstd_done")
    scaled = sem("scaled")
    rt_ready = sem("rt_ready")
    consts = sem("consts")
    ws_loaded = sem("ws_loaded")
    rope_loaded = sem("rope_loaded")
    ident_done = sem("ident_done")
    ws_masked = sem("ws_masked")
    sink_loaded = sem("sink_loaded")
    bs_loaded = sem("bs_loaded")
    gain_step = sem("gain_step")
    split_step = sem("split_step")
    vbias_loaded = [sem(f"vbias_loaded{e}") for e in range(2)]
    v_biased = sem("v_biased")
    v_counted = sem("v_counted")
    v_act = sem("v_act")
    vT_back = sem("vT_back")
    x_loaded = [sem(f"x_loaded{m}") for m in range(4)]
    v_parked = sem("v_parked")
    v_stat = sem("v_stat")
    v_root = sem("v_root")
    ln_step = sem("ln_step")
    bias_done = sem("bias_done")
    q_copied = sem("q_copied")
    rope_step = sem("rope_step")
    q_done = sem("q_done")
    vT_copied = sem("vT_copied")
    v_copied = sem("v_copied")
    q_staged = sem("q_staged")
    v_staged = sem("v_staged")
    s_full = sem("s_full")
    s_max = sem("s_max")
    s_exp = sem("s_exp")
    s_norm = sem("s_norm")
    p_full = sem("p_full")
    p_copied = sem("p_copied")
    o_full = sem("o_full")
    o_hi = sem("o_hi")
    o_lo = sem("o_lo")

    def f(ap):
        return ap.bitcast(F32)

    def in_tile(t, b):
        v = t[:, :].rearrange("p (k f) -> p k f", k=KT)
        return lambda k: v[:, k, b * P:(b + 1) * P]

    with nc.Block() as block:
        @block.sync
        def _(sp):
            def load_in(s, use, src, first=False):
                if not first:
                    sp.wait_ge(w_ready[s], use)
                sp.dma_start(raw[s][:, :].rearrange("p (k f) -> p k f", k=KT),
                             src.rearrange("(k p) f -> p k f", p=P)).then_inc(loaded[s], 16)

            def load_down(use, src, first=False):
                if not first:
                    sp.wait_ge(w_ready[W2], use)
                sp.dma_start(raw[W2][:, :].rearrange("p (t n) -> p t n", t=2),
                             src.rearrange("(t p) n -> p t n", p=P)).then_inc(loaded[W2], 16)

            def norm_loads(n):
                sp.dma_start(gpost[:, :], post_gain[n].to_broadcast([P, D])).then_inc(g_loaded, 16)
                for m in range(2):
                    sp.dma_start(hin[:, m, :], h_from[n][m]).then_inc(h_loaded[m], 16)

            def norm_tile(n, m, par, more):
                sp.wait_ge(h_new, TT * (n - 1) + m + 1)
                sp.dma_start(h_to[n][ds(m, 1)].rearrange("a p d -> (a p) d"), hout[:, par, :]).then_inc(h_stored[par], 16)
                if more:
                    sp.dma_start(hin[:, par, :], h_from[n][ds(m + 2, 1)].rearrange("a p d -> (a p) d")).then_inc(h_loaded[par], 16)

            def norm(n, between=lambda: None):
                for m in range(TT // 2):
                    norm_tile(n, m, m % 2, True)
                between()
                with sp.Fori(TT // 4, TT // 2 - 1) as j:
                    for par in range(2):
                        norm_tile(n, j * 2 + par, par, True)
                for m in (TT - 2, TT - 1):
                    norm_tile(n, m, m % 2, False)

            def ffn(layer):
                use = (USE_FFN0, USE_FFN1)[layer]
                gu, down = f_w_gate_up[layer], f_w_down[layer]

                def chunk(c):
                    load_in(G, use[G] + c, gu[:, ds(c * PAIR, PAIR)])
                    load_in(U, use[U] + c, gu[:, ds(c * PAIR + D_FF, PAIR)], first=layer == 0 and isinstance(c, int) and c == 0)
                    load_down(use[W2] + c, down[ds(c * PAIR, PAIR), :])
                return chunk

            rows = sg[:, 0, 0:P]
            srcs = [norm_mix_pre[0], norm_mix_pre[1], norm_ffn_pre[0], norm_ffn_pre[1], kv_norm, a_b_in[0][0:GMLP_HALF]]
            at = 0
            for src in srcs:
                r = src.rearrange("(k p) -> k p", p=P)
                sp.dma_start(rows[at:at + r.shape[0], :], r).then_inc(consts, 16)
                at += r.shape[0]
            def load_x(m):
                if m >= 4:
                    sp.wait_ge(rt_ready, m - 3)
                sp.dma_start(x_tile(m), x_in[m]).then_inc(x_loaded[m % 4], 16)

            for m in range(4):
                load_x(m)
            w_in = a_w_in[0]

            def load_vbias(p, e):
                sp.dma_start(vbias[:, e, :], a_b_in[0:1, ds(p * -PAIR + (GMLP_FFN - PAIR), PAIR)].to_broadcast([P, PAIR])).then_inc(vbias_loaded[e], 16)

            load_in(G, 0, w_in[:, GMLP_FFN - PAIR:GMLP_FFN], first=True)
            for m in range(4, TT):
                load_x(m)
            for e in range(2):
                load_vbias(e, e)
            load_in(W2, 0, w_in[:, GMLP_FFN - 2 * PAIR:GMLP_FFN - PAIR], first=True)
            sp.dma_start(gpost[:, :].rearrange("p (g j) -> p g j", g=GROUPS),
                         a_w_s[0].rearrange("g i j -> i g j")).then_inc(ws_loaded, 16)
            for g in range(NKV):
                for t in range(2):
                    sp.dma_start(sink[t * HEAD:(t + 1) * HEAD, g, :],
                                 b_sinks[0:1, g * 8 + t:(g + 1) * 8:2].to_broadcast([HEAD, NPAIR]),
                                 allow_slow_non_contiguous=True).then_inc(sink_loaded, 16)
            sp.wait_ge(rt_ready, TT)
            sp.dma_start(bs[:, :, :].rearrange("p g i -> p (g i)"),
                         a_b_s[0:1].rearrange("a g i -> a (g i)").to_broadcast([P, D])).then_inc(bs_loaded, 16)

            def load_ln(g):
                for e, src in enumerate((a_ln_g, a_ln_b)):
                    sp.dma_start(lngb[:, e, :], src[0:1, ds(g * PAIR, PAIR)].to_broadcast([P, PAIR])).then_inc(loaded[U], 16)

            load_ln(0)

            def park_v(p):
                sp.wait_ge(v_act, p * 4 + 4)
                sp.dma_start(v_dram[ds(p * -1 + (GMLP_CHUNKS - 2), 1)].rearrange("a p n -> (a p) n"), raw[U][:, :]).then_inc(v_parked, 16)

            with sp.Fori(0, GROUPS // 2 - 1) as i:
                for e, s in enumerate((G, W2)):
                    load_in(s, i + 1, w_in[:, ds(i * (-2 * PAIR) + (GMLP_FFN - (3 + e) * PAIR), PAIR)])
                    park_v(i * 2 + e)
                    load_vbias(i * 2 + (2 + e), e)
            load_in(G, USE_GMLP[G], w_in[:, 0:PAIR])
            park_v(GMLP_CHUNKS - 2)
            load_down(USE_GMLP[W2], a_w_out[0, 0:PAIR, :])

            def load_v(g):
                sp.dma_start(raw[U][:, :], v_dram[ds(g - 1, 1)].rearrange("a p n -> (a p) n")).then_inc(loaded[U], 16)
                load_ln(g)

            sp.wait_ge(v_parked, 16 * (GMLP_CHUNKS - 1))
            with sp.Fori(1, GMLP_CHUNKS) as g:
                load_in(G, g + USE_GMLP[G], w_in[:, ds(g * PAIR, PAIR)])
                sp.wait_ge(normed_v, g)
                load_v(g)
                load_down(g + USE_GMLP[W2], a_w_out[0, ds(g * PAIR, PAIR), :])

            chunk = ffn(0)
            sp.wait_ge(normed_v, GMLP_CHUNKS)
            chunk(0)
            sp.wait_ge(prod_ready, 2 * 2 * GMLP_CHUNKS)
            norm_loads(1)
            norm(1)
            with sp.Fori(1, FFN_CHUNKS) as c:
                chunk(c)

            def load_q(s, use, j):
                sp.wait_ge(w_ready[s], use)
                for b in range(2):
                    for g in range(NKV):
                        dst = raw[s][:, :].rearrange("p (k b g f) -> p k b g f", k=KT, b=2, g=NKV)[:, :, b, g, :]
                        at = (g * 8 + j * 2 + b) * HEAD
                        src = b_w_q[0][:, at:at + HEAD].rearrange("(k p) f -> p k f", p=P)
                        sp.dma_start(dst, src).then_inc(loaded[s], 16)

            load_in(G, USE_KV[G], w_kv)
            load_q(U, USE_Q[U], 0)
            for par in range(2):
                sp.wait_ge(h_stored[par], 16 * (TT // 2))
            norm_loads(2)

            def more_loads():
                load_q(G, USE_Q[G], 1)
                sp.wait_ge(down_full, DOWN_BANKS * DOWN_O)
                sp.dma_start(cosT[:, :], rope_cos).then_inc(rope_loaded, 16)
                sp.dma_start(sinT[:, :], rope_sin).then_inc(rope_loaded, 16)

            norm(2, more_loads)
            for j in range(2, Q_PAIRS):
                load_q((U, G)[j % 2], (USE_Q[U], USE_Q[G])[j % 2] + j // 2, j)

            def load_o(j):
                s = (W2, U)[j % 2]
                if j:
                    sp.wait_ge(w_ready[s], USE_O[s] + j // 2)
                else:
                    sp.wait_ge(q_done, 2 + 2 * (D // P))
                for g in range(NKV):
                    dst = raw[s][g * HEAD:(g + 1) * HEAD, :].rearrange("p (t n) -> p t n", t=2)
                    lo = g * 512 + j * 2 * HEAD
                    src = b_w_o[0][lo:lo + 2 * HEAD, :].rearrange("(t p) n -> p t n", p=HEAD)
                    sp.dma_start(dst, src).then_inc(loaded[s], 16)

            for j in range(Q_PAIRS):
                load_o(j)
            sp.wait_ge(o_full, NKV * NCHUNK)
            norm_loads(3)
            chunk = ffn(1)
            chunk(0)
            norm(3)
            with sp.Fori(1, FFN_CHUNKS) as c:
                chunk(c)
            for par in range(2):
                sp.wait_ge(h_stored[par], 16 * (TT // 2) * 3)
            norm_loads(4)
            norm(4)
            for par in range(2):
                sp.wait_ge(h_stored[par], 16 * (TT // 2) * 4)

        @block.gpsimd
        def _(pool):
            total = {"gain": 0, "split": 0}

            def body(i, rounds, uses):
                gains, done = KT * sum(u[3] is not None for u in uses), 0
                for n, (s, use, data, gain, free) in enumerate(uses):
                    pool.wait_ge(*data)
                    if gain is not None:
                        pool.nop(nofuse=True)
                        for k in range(KT):
                            r = raw[s][:, k * PAIR:(k + 1) * PAIR]
                            nc.gpsimd.tensor_scalar(r, r, cols[:, gain + k:gain + k + 1], 0.0, ALU.mult, ALU.add).then_inc(gain_step, 1)
                        done += KT
                        pool.wait_ge(gain_step, i * gains + (total["gain"] + done))
                    if free is not None:
                        pool.wait_ge(*free)
                    pool.nop(nofuse=True)
                    nc.gpsimd.tensor_scalar(WH[s][:, :], raw[s][:, :], 1.0, 0.0, ALU.mult, ALU.add).then_inc(split_step, 1)
                    pool.wait_ge(split_step, i * len(uses) + (total["split"] + n + 1))
                    nc.gpsimd.tensor_tensor(WL[s][:, :], raw[s][:, :], f(WH[s][:, :]), ALU.subtract).then_inc(w_ready[s], 1)
                total["gain"] += gains * rounds
                total["split"] += len(uses) * rounds

            nc.gpsimd.memset(ident[:, :], 0.0).then_inc(pool_step, 1)
            pool.wait_ge(pool_step, 1)
            nc.gpsimd.affine_select(out=ident[:, :], in_=ident[:, :], compare_op=ALU.not_equal, fill=1.0,
                                    base=0, pattern=[[-1, P]], channel_multiplier=1).then_inc(ident_done, 1)

            def zero_acc(n):
                for m in range(TT):
                    pool.wait_ge(tr_full, TR_NORM(n) + 2 * m + 2)
                    nc.gpsimd.memset(acc[:, m, :], 0.0).then_inc(acc_zero, 1)

            pool.wait_ge(tr_free, 1)
            gm = GAIN_MIX[0]
            body(0, 1, [(s, 0, (loaded[s], 16), gm, None) for s in (G, W2)])
            zero_acc(0)
            with pool.Fori(0, GROUPS // 2 - 1) as i:
                body(i, GROUPS // 2 - 1, [(s, i + 1, (loaded[s], i * 16 + 32), gm, (proj_full, i * 8 + v))
                                           for s, v in ((G, 4), (W2, 8))])

            def gmlp(g, frees):
                return [(G, g + USE_GMLP[G], (loaded[G], (g + USE_GMLP[G]) * 16 + 16), gm, frees[0]),
                        (W2, g + USE_GMLP[W2], (loaded[W2], (g + USE_GMLP[W2]) * 16 + 16), None, frees[1])]
            body(0, 1, gmlp(0, ((proj_full, V_PIECES - 4), (proj_full, V_PIECES))))
            with pool.Fori(0, GMLP_CHUNKS - 1) as i:
                body(i, GMLP_CHUNKS - 1, gmlp(i + 1, ((act_full, i * 4 + 4),
                                                      (down_full, i * 2 * DOWN_BANKS + 2 * DOWN_BANKS))))

            loads_ffn0 = (USE_FFN0[G], 3 * GMLP_CHUNKS - 1, USE_FFN0[W2])
            loads_kv = tuple(n + FFN_CHUNKS for n in loads_ffn0)
            loads_q = (loads_kv[0] + 1, loads_kv[1], loads_kv[2])
            loads_o = (loads_q[0] + 2 * Q_PAIRS, loads_q[1] + 2 * Q_PAIRS, loads_q[2])
            loads_ffn1 = (loads_o[0], loads_o[1] + Q_PAIRS, loads_o[2] + Q_PAIRS)

            def ffn(layer, n, before):
                use, loads = ((USE_FFN0, loads_ffn0), (USE_FFN1, loads_ffn1))[layer]
                st, dn, gain = STAGE_FFN[layer], (DOWN_FFN0, DOWN_FFN1)[layer], GAIN_FFN[layer]

                def uses(c, frees):
                    return [(s, c + use[s], (loaded[s], c * 16 + 16 * (loads[s] + 1)), g, frees[s])
                            for s, g in ((G, gain), (U, gain), (W2, None))]
                body(0, 1, uses(0, before))
                zero_acc(n)
                with pool.Fori(0, FFN_CHUNKS - 1) as i:
                    body(i, FFN_CHUNKS - 1, uses(i + 1, ((act_full, i * 4 + (2 * st + 4)), (mul_full, i * 4 + (2 * st + 4)),
                                                         (down_full, i * 2 * DOWN_BANKS + (dn + 2) * DOWN_BANKS))))

            ffn(0, 1, ((act_full, 2 * STAGE_FFN[0]), (mul_full, 2 * STAGE_FFN[0]), (down_full, DOWN_BANKS * DOWN_FFN0)))
            end_ffn0 = 2 * STAGE_FFN[1]
            body(0, 1, [(G, USE_KV[G], (loaded[G], 16 * (loads_kv[G] + 1)), GAIN_KV, (act_full, end_ffn0))])
            for j in range(Q_PAIRS):
                s = (U, G)[j % 2]
                free = (mul_full, end_ffn0) if j == 0 else (proj_full, PROJ_Q + 4 * (j - 1))
                body(0, 1, [(s, USE_Q[s] + j // 2, (loaded[s], 16 * (loads_q[s] + 4 * (j // 2 + 1))), GAIN_MIX[1], free)])

            def stage_q(n, par):
                if not isinstance(n, int) or n > 1:
                    wait_apart(pool, s_full, n * NKV - NKV)
                nc.gpsimd.tensor_copy(qc[par][:, :], qT[:, ds(n * KT * CHUNK, KT * CHUNK)]).then_inc(q_staged, 1)

            def stage_v(n, par, m):
                if not isinstance(n, int) or n > 1:
                    wait_apart(pool, o_full, n * NKV - NKV)
                src = (vshift, vt)[par][:, ds(m, 1), :].rearrange("p a n -> p (a n)")
                for kv in range(NKV):
                    d = slice(kv * HEAD, (kv + 1) * HEAD)
                    op = nc.gpsimd.tensor_copy(vc[par][kv][:, d], src[:, d])
                op.then_inc(v_staged, 1)

            pool.wait_ge(q_done, 2 + 2 * (D // P) - 2)
            pool.wait_ge(v_copied, 2)
            pool.wait_ge(proj_full, PROJ_END)
            stage_q(0, 0)
            for e in range(2):
                for kv in range(NKV):
                    nc.gpsimd.memset(vc[e][kv][:, (1 - kv) * HEAD:(2 - kv) * HEAD], 0.0)
            stage_q(1, 1)
            stage_v(0, 0, 0)
            stage_q(2, 0)
            stage_v(1, 1, 0)
            pool.wait_ge(q_done, 2 + 2 * (D // P))
            with pool.Fori(1, NCHUNK // 2 - 1) as m:
                stage_q(m * 2 + 1, 1)
                stage_v(m * 2, 0, m)
                stage_q(m * 2 + 2, 0)
                stage_v(m * 2 + 1, 1, m)
            stage_q(NCHUNK - 1, 1)
            for n in (NCHUNK - 2, NCHUNK - 1):
                stage_v(n, n % 2, n // 2)

            for j in range(Q_PAIRS):
                s = (W2, U)[j % 2]
                free = (proj_full, PROJ_Q + 12) if j == 1 else (down_full, DOWN_BANKS * (DOWN_O + 2 * max(j - 1, 0)))
                body(0, 1, [(s, USE_O[s] + j // 2, (loaded[s], 16 * (loads_o[s] + 2 * (j // 2 + 1))), None, free)])
            ffn(1, 3, ((o_full, NKV * NCHUNK), (down_full, DOWN_BANKS * DOWN_FFN1), (down_full, DOWN_BANKS * (DOWN_FFN1 - 1))))

        @block.tensor
        def _(pe):
            def pair3(dst, wh, wl, xh, xl, first, last):
                nc.tensor.matmul(dst, wh, xh, start=first, stop=False)
                nc.tensor.matmul(dst, wh, xl, start=False, stop=False)
                return nc.tensor.matmul(dst, wl, xh, start=False, stop=last)

            def project(dst, s, tile, b, half, midway=None):
                wh, wl = tile(WH[s], b), tile(WL[s], b)
                for k in range(KT):
                    if midway is not None and k == KT // 2:
                        midway()
                    t = slice(half * HALF, (half + 1) * HALF)
                    mm = pair3(dst, wh(k), wl(k), XH[:, k, t], XL[:, k, t], k == 0, k == KT - 1)
                return mm

            def down(n, half_of_x=None, x_pair=None, s=W2):
                for m in range(4):
                    for o in range(2):
                        q = m * 2 + o
                        if not (isinstance(n, int) and n * DOWN_BANKS + q < 2):
                            pe.wait_ge(down_added, n * DOWN_BANKS + (q - 1))
                        dst = bank[4 + q % 2][:, :]
                        for t in range(2):
                            if x_pair is None:
                                lh, ll = hidH[:, t, m * P:(m + 1) * P], hidL[:, t, m * P:(m + 1) * P]
                            else:
                                tok = slice(half_of_x * HALF + m * P, half_of_x * HALF + (m + 1) * P)
                                lh, ll = XH[:, x_pair + t, tok], XL[:, x_pair + t, tok]
                            c = slice(t * D + o * HALF, t * D + (o + 1) * HALF)
                            nc.tensor.matmul(dst, lh, WH[s][:, c], start=(t == 0), stop=False)
                            nc.tensor.matmul(dst, lh, WL[s][:, c], start=False, stop=False)
                            mm = nc.tensor.matmul(dst, ll, WH[s][:, c], start=False, stop=(t == 1))
                        mm.then_inc(down_full, 1)

            def transposes(src, dst):
                for q in range(4):
                    mm = nc.tensor.transpose(dst[:, q * P:(q + 1) * P], src[:, q * P:(q + 1) * P], ident[:, :])
                return mm

            def norm_tile(n, m):
                pe.wait_ge(rt_ready, m + (TT * n + 1))
                for q in range(2):
                    before = m * 2 + TR_NORM(n) + q - 1
                    pe.wait_ge(tr_free, max(before, TR_COLS))
                    transposes(acc[:, m, q * HALF:(q + 1) * HALF], bank[6 + q]).then_inc(tr_full, 1)

            def x_ready(n, half):
                pe.wait_ge(tr_free, TR_NORM(n) + TT * (half + 1))

            def stage_ins(stage, half, s, full, first_bank, after=lambda b: None):
                free = act_ready if first_bank == 0 else prod_ready
                for b in range(2):
                    if not (isinstance(stage, int) and stage == 0):
                        pe.wait_ge(free, stage * 2 + (b - 1))
                    project(bank[first_bank + b][:, :], s, in_tile, b, half).then_inc(full, 1)
                    after(b)

            def hidden_ready(stage):
                pe.wait_ge(hid_hi, stage * 2 + 2)
                pe.wait_ge(hid_lo, stage * 2 + 2)

            def mix(stage, group, half):
                wg = wsT[:, ds(group, 1), :].rearrange("p a i -> p (a i)")
                for b in range(2):
                    if not (isinstance(stage, int) and stage == 0):
                        pe.wait_ge(prod_ready, stage * 2 + (b - 1))
                    for q in range(4):
                        m = half * 4 + q
                        dst = bank[2 + b][:, q * P:(q + 1) * P]
                        mm = nc.tensor.matmul(dst, vn[:, m, b * P:(b + 1) * P], wg, start=True, stop=True)
                    mm.then_inc(mul_full, 1)

            def ffn_chunk(layer, c, first):
                use = (USE_FFN0, USE_FFN1)[layer]
                base, dbase = STAGE_FFN[layer], (DOWN_FFN0, DOWN_FFN1)[layer]
                n = 2 * layer + 1
                for h in range(2):
                    st = c * 2 + (base + h)
                    with_norm = first and h == 0
                    if h == 0:
                        pe.wait_ge(w_ready[G], c + (use[G] + 1))
                    stage_ins(st, h, G, act_full, 0, (lambda b: norm_tile(n, 4 + b)) if with_norm else lambda b: None)
                    if not (first and h == 0):
                        down_step(c * 2 + (base + h - 1), c * 2 + (dbase + h - 1), use, c, h)
                    if h == 0:
                        pe.wait_ge(w_ready[U], c + (use[U] + 1))
                    stage_ins(st, h, U, mul_full, 2, (lambda b: norm_tile(n, 6 + b)) if with_norm else lambda b: None)
                    if with_norm:
                        x_ready(n, 1)

            def down_step(stage, n, use, c, h):
                hidden_ready(stage)
                if h == 1:
                    pe.wait_ge(w_ready[W2], c + (use[W2] + 1))
                down(n)

            def gmlp_chunk(g, first):
                for h in range(2):
                    st = g * 2 + h
                    if h == 0:
                        pe.wait_ge(w_ready[G], g + (USE_GMLP[G] + 1))
                    stage_ins(st, h, G, act_full, 0)
                    if not (first and h == 0):
                        down_step(g * 2 + (h - 1), g * 2 + (h - 1), USE_GMLP, g, h)
                    if h == 0:
                        pe.wait_ge(normed_v, g + 1)
                    mix(st, g, h)

            pe.wait_ge(consts, 16 * 6)
            pe.wait_ge(ident_done, 1)
            nc.tensor.transpose(bank[6][:, 0:NCOLS], sg[0:NCOLS, 0, 0:P], ident[0:NCOLS, 0:NCOLS]).then_inc(tr_full, 1)
            for m in range(TT // 2):
                norm_tile(0, m)
            x_ready(0, 0)

            def w_s_back():
                pe.wait_ge(ws_masked, 1)
                for q in range(2):
                    pe.wait_ge(tr_free, TR_WS + q - 1)
                    transposes(gpost[:, q * HALF:(q + 1) * HALF], bank[6 + q]).then_inc(tr_full, 1)

            def v_pair(i, s, e, first):
                pe.wait_ge(w_ready[s], i + 1)
                wh, wl = [t[s][:, :].rearrange("p (k f) -> p k f", k=KT) for t in (WH, WL)]
                for q in range(4):
                    idx = i * 8 + (4 * e + q)
                    early = first and e == 0 and q < 2
                    if first and e == 0 and q == 2:
                        x_ready(0, 1)
                    if not (first and e == 0):
                        pe.wait_ge(v_biased, idx - 3)
                    for t in range(2):
                        m = 2 * q + t
                        tok = slice(m * P, (m + 1) * P)
                        dst = bank[q][:, t * PAIR:(t + 1) * PAIR]
                        for k in range(KT):
                            nc.tensor.matmul(dst, XH[:, k, tok], wh[:, k, :], start=(k == 0), stop=False)
                            nc.tensor.matmul(dst, XH[:, k, tok], wl[:, k, :], start=False, stop=False)
                            mm = nc.tensor.matmul(dst, XL[:, k, tok], wh[:, k, :], start=False, stop=(k == KT - 1))
                        if t == 1:
                            mm.then_inc(proj_full, 1)
                        if early:
                            norm_tile(0, 4 + m)
                    if first and e == 0 and q == 2:
                        w_s_back()

            for e, s in enumerate((G, W2)):
                v_pair(0, s, e, True)
            with pe.Fori(1, GROUPS // 2) as i:
                for e, s in enumerate((G, W2)):
                    v_pair(i, s, e, False)

            pe.wait_ge(v_biased, V_PIECES - 2)
            gmlp_chunk(0, True)
            with pe.Fori(1, GMLP_CHUNKS) as g:
                gmlp_chunk(g, False)

            def ffn(layer, n):
                ffn_chunk(layer, 0, True)
                with pe.Fori(1, FFN_CHUNKS) as c:
                    ffn_chunk(layer, c, False)

            def last_down(stage, n, norm):
                if norm == 2:
                    norm_tile(norm, 0)
                hidden_ready(stage)
                down(n)
                if norm < 4:
                    for m in range(1 if norm == 2 else 0, TT // 2):
                        norm_tile(norm, m)
                    x_ready(norm, 0)

            last_down(STAGE_FFN[0] - 1, DOWN_FFN0 - 1, 1)
            ffn(0, 1)
            last_down(STAGE_FFN[1] - 1, DOWN_O - 1, 2)
            pe.wait_ge(w_ready[G], USE_KV[G] + 1)
            for h in range(2):
                if h:
                    x_ready(2, 1)
                for b in range(2):
                    project(bank[2 * b + h][:, :], G, in_tile, b, h,
                            midway=None if h else lambda: norm_tile(2, 4 + 2 * b)).then_inc(proj_full, 1)
                    if h == 0:
                        norm_tile(2, 5 + 2 * b)
            for j in range(Q_PAIRS):
                s = (U, G)[j % 2]
                pe.wait_ge(w_ready[s], USE_Q[s] + j // 2 + 1)
                for h in range(2):
                    for b in range(2):
                        q = 4 * j + 2 * h + b
                        if q in (2, 3):
                            pe.wait_ge(vT_copied, q - 1)
                        else:
                            pe.wait_ge(q_copied, q + 1 if q < 2 else q - 1)
                        project(bank[2 * h + b][:, :], s, in_tile, b, h).then_inc(proj_full, 1)
                        if q == 1:
                            for half in range(2):
                                pe.wait_ge(vT_copied, half + 1)
                                transposes(sg[:, half, :], bank[6 + half]).then_inc(vT_back, 1)

            def scores(n, par, kv):
                u = n * NKV + kv
                first = isinstance(n, int) and n == 0
                if not first:
                    pe.wait_ge(s_exp, u - 1)
                lo = CHUNK if first else 0
                keys = slice(0, CHUNK) if first else ds(n * CHUNK - CHUNK, P)
                if kv == 0:
                    pe.wait_ge(q_staged, n + 1)
                for j in range(NPAIR):
                    mm = nc.tensor.matmul(bank[kv][:, j * P + lo:(j + 1) * P], qc[par][:, j * P:(j + 1) * P],
                                          kz[kv][:, keys], start=True, stop=True)
                mm.then_inc(s_full, 1)

            def probs_back(n, kv):
                u = n * NKV + kv
                pe.wait_ge(s_norm, u * 3 + 3)
                if not (isinstance(n, int) and n == 0):
                    pe.wait_ge(p_copied, u - 1)
                for j in range(NPAIR):
                    mm = nc.tensor.transpose(bank[6 + kv][:, j * P:(j + 1) * P], prob[kv][:, j, :], ident[:, :])
                mm.then_inc(p_full, 1)

            def values(n, par, kv):
                u = n * NKV + kv
                pe.wait_ge(p_copied, u + 1)
                if kv == 0:
                    pe.wait_ge(v_staged, n + 1)
                    if not (isinstance(n, int) and n < 2):
                        pe.wait_ge(o_lo, n - 1)
                nc.tensor.matmul(bank[2 + par][:, :], vc[par][kv][:, :], pT[kv][:, :], start=(kv == 0),
                                 stop=(kv == NKV - 1)).then_inc(o_full, 1)

            def attend(n, par):
                known = isinstance(n, int)
                for kv in range(NKV):
                    if not known or n < NCHUNK:
                        scores(n, par, kv)
                    if not known or n >= 2:
                        values(n - 2, par, kv)
                    if not known or 1 <= n <= NCHUNK:
                        probs_back(n - 1, kv)

            for n in range(4):
                attend(n, n % 2)
            with pe.Fori(2, NCHUNK // 2) as m:
                attend(m * 2, 0)
                attend(m * 2 + 1, 1)
            attend(NCHUNK, 0)
            attend(NCHUNK + 1, 1)

            pe.wait_ge(o_lo, NCHUNK)
            for i, (j, h) in enumerate(O_ORDER):
                s = (W2, U)[j % 2]
                if h == 0:
                    pe.wait_ge(w_ready[s], USE_O[s] + j // 2 + 1)
                down(DOWN_O + i, half_of_x=h, x_pair=2 * j, s=s)
                if i == len(O_ORDER) - 2:
                    norm_tile(3, 0)
            for m in (1, 2, 3):
                norm_tile(3, m)
            x_ready(3, 0)
            ffn(1, 3)
            last_down(STAGES - 1, DOWN_END - 1, 4)

        @block.scalar
        def _(act):
            def x_hi(n, m):
                for q in range(2):
                    wait_apart(act, tr_full, m * 2 + (TR_NORM(n) + q + 1))
                    nc.scalar.activation(XH[:, 4 * q:4 * q + 4, ds(m * P, P)],
                                         bank[6 + q][:, :].rearrange("p (k t) -> p k t", k=4),
                                         ACT.Copy).then_inc(tr_hi, 1)

            def norm_step(n, k, par, has1, has2, has3):
                pre = n < 4
                base_step = STEP_BASE[n]
                one, two = has1, has2 and pre
                if one or two:
                    wait_apart(act, ms_done, k + base_step)
                if one:
                    op = nc.scalar.activation(junk[:, :], acc[:, ds(k, 1), :].rearrange("p a n -> p (a n)"),
                                              ACT.Square, accum_out=ssq[:, 0:1])
                if two:
                    other = 1 - par
                    wait_apart(act, h_new, k + TT * (n - 1))
                    op = nc.scalar.activation(acc[:, ds(k - 1, 1), :].rearrange("p a n -> p (a n)"), hout[:, other, :],
                                              ACT.Square, accum_out=ssq[:, 1:2])
                if one or two:
                    op.then_inc(sq_done, 1)
                    c = slice(0 if one else 1, 2 if two else 1)
                    act.wait_ge(ms_done, k + (base_step + 1))
                    nc.scalar.activation(root[:, c], rms[:, c], ACT.Sqrt).then_inc(root_done, 1)
                if has3 and pre:
                    x_hi(n, k - 2)

            def first_steps(n, steps):
                for k in steps:
                    norm_step(n, k, k % 2, True, k > 0, k > 1)

            def last_steps(n):
                act.wait_ge(down_added, DOWN_BANKS * DOWN_BEFORE_NORM[n])
                with act.Fori(TT // 4, TT // 2) as j:
                    norm_step(n, j * 2, 0, True, True, True)
                    norm_step(n, j * 2 + 1, 1, True, True, True)
                if n < 4:
                    norm_step(n, TT, 0, False, True, True)
                    norm_step(n, TT + 1, 1, False, False, True)

            def x_square(m):
                act.wait_ge(x_loaded[m % 4], 16 * (m // 4 + 1))
                nc.scalar.activation(acc[:, m, :], x_tile(m), ACT.Square, accum_out=x_ssq[:, m:m + 1]).then_inc(sq_done, 1)

            def x_roots(b, tiles):
                c = slice(tiles[0], tiles[-1] + 1)
                act.wait_ge(ms_done, b + 1)
                nc.scalar.activation(x_root[:, c], x_ms[:, c], ACT.Sqrt).then_inc(root_done, 1)

            for b in range(2):
                for m in X_BATCHES[b]:
                    x_square(m)
                x_roots(b, X_BATCHES[b])
            for m in range(TT // 2):
                x_hi(0, m)
                x_square(4 + m)
            x_roots(2, X_BATCHES[2])
            for m in range(TT // 2, TT):
                x_hi(0, m)

            def v_gelu(i, q, first):
                idx = i * 8 + q
                act.wait_ge(v_biased, idx + 1)
                if q % 4 == 0 and not (first and q == 0):
                    act.wait_ge(v_parked, i * 32 + 4 * q)
                act.nop(nofuse=True)
                nc.scalar.activation(raw[U][:, (q % 4) * HALF:(q % 4 + 1) * HALF], sg[:, q % 2, :],
                                     ACT.Gelu_apprx_tanh).then_inc(v_act, 1)

            for q in range(8):
                v_gelu(0, q, True)
            with act.Fori(1, GROUPS // 2) as i:
                for q in range(8):
                    v_gelu(i, q, False)
            act.wait_ge(v_stat, 2)
            nc.scalar.activation(vrstd[:, :], vrstd[:, :], ACT.Sqrt).then_inc(v_root, 1)

            def stage(st, func, bias, first=False, between=lambda: None):
                for b in range(2):
                    act.wait_ge(act_full, st * 2 + (b + 1))
                    if not first:
                        act.wait_ge(hid_lo, st * 2 + (b - 1))
                    act.nop(nofuse=True)
                    if bias is None:
                        nc.scalar.activation(sg[:, b, :], bank[b][:, :], func).then_inc(act_ready, 1)
                    else:
                        nc.scalar.activation(sg[:, b, :], bank[b][:, :], func, bias=bias(b)).then_inc(act_ready, 1)

                between()
                for b in range(2):
                    act.wait_ge(prod_ready, st * 2 + (b + 1))
                    nc.scalar.activation(hidH[:, b, :], sg[:, b, :], ACT.Copy).then_inc(hid_hi, 1)

            def gmlp(g, first):
                for h in range(2):
                    stage(g * 2 + h, ACT.Gelu_apprx_tanh, lambda b: cols[:, ds(g * 2 + (BIAS_IN + b), 1)], first and h == 0)

            gmlp(0, True)
            with act.Fori(1, GMLP_CHUNKS) as g:
                gmlp(g, False)

            def early_steps(n):
                act.wait_ge(down_added, DOWN_BANKS * (DOWN_BEFORE_NORM[n] - 1))
                first_steps(n, (0, 1))

            def ffn(layer):
                n = 2 * layer + 2
                with act.Fori(0, 2 * FFN_CHUNKS - 1) as c:
                    stage(c + STAGE_FFN[layer], ACT.Silu, None)
                stage(STAGE_FFN[layer] + 2 * FFN_CHUNKS - 1, ACT.Silu, None, between=lambda: early_steps(n))
                first_steps(n, (2, 3))
                last_steps(n)

            early_steps(1)
            first_steps(1, (2, 3))
            last_steps(1)
            ffn(0)

            def plain_and_rotated(r, full, src):
                e = r % 2
                act.wait_ge(proj_full, full)
                if r >= 2:
                    act.wait_ge(q_done, r - 1)
                nc.scalar.activation(qplain[e], src[:, :], ACT.Copy)
                for q in range(4):
                    a, b = q * 32, (q ^ 1) * 32
                    op = nc.scalar.activation(qrot[e][a:a + 32, :], src[b:b + 32, :], ACT.Copy)
                op.then_inc(q_copied, 1)

            for h in range(2):
                plain_and_rotated(h, PROJ_KV + 2 * h + 1, bank[h])
                act.wait_ge(proj_full, PROJ_KV + 2 * h + 2)
                nc.scalar.activation(sg[:, h, :], bank[2 + h][:, :], ACT.Copy).then_inc(vT_copied, 1)
            plain_and_rotated(2, PROJ_Q + 1, bank[0])
            for h in range(2):
                act.wait_ge(vT_back, h + 1)
                src = bank[6 + h][:, :].rearrange("p (m d) -> p m d", m=4)
                after = min(4, TT - 1 - 4 * h)
                nc.scalar.activation(vshift[CHUNK:P, 4 * h:4 * h + 4, :], src[0:CHUNK], ACT.Copy)
                nc.scalar.activation(vshift[0:CHUNK, 4 * h + 1:4 * h + 1 + after, :], src[CHUNK:P, 0:after, :], ACT.Copy)
                nc.scalar.activation(vt[:, 4 * h:4 * h + 4, :], src, ACT.Copy).then_inc(v_copied, 1)
            for q in range(1, 2 * (D // P)):
                plain_and_rotated(2 + q, PROJ_Q + q + 1, bank[q % 4])

            def exps(n, kv):
                u = n * NKV + kv
                first = isinstance(n, int) and n == 0
                act.wait_ge(s_max, u * 3 + 3)
                if not first:
                    act.wait_ge(p_full, u - 1)
                lo = CHUNK if first else 0
                nc.scalar.activation(a_snk[:, kv, :], a_off[:, kv, :], ACT.Exp)
                for j in range(NPAIR):
                    op = nc.scalar.activation(prob[kv][:, j, lo:P], bank[kv][:, j * P + lo:(j + 1) * P], ACT.Exp,
                                              bias=a_neg[:, kv, j:j + 1], scale=SCALE, accum_out=a_sum[:, kv, j:j + 1])
                op.then_inc(s_exp, 1)

            def p_copy(n, kv):
                u = n * NKV + kv
                act.wait_ge(p_full, u + 1)
                if not (isinstance(n, int) and n == 0):
                    act.wait_ge(o_full, u - 1)
                nc.scalar.activation(pT[kv][:, :], bank[6 + kv][:, :], ACT.Copy).then_inc(p_copied, 1)

            def o_split(n, par):
                wait_apart(act, o_full, n * NKV + NKV)
                nc.scalar.activation(XH[:, :, ds(n * CHUNK, CHUNK)],
                                     bank[2 + par][:, :].rearrange("p (t c) -> p t c", t=KT), ACT.Copy).then_inc(o_hi, 1)

            def attend(n, par):
                known = isinstance(n, int)
                for kv in range(NKV):
                    if not known or 1 <= n <= NCHUNK:
                        p_copy(n - 1, kv)
                    if not known or n < NCHUNK:
                        exps(n, kv)
                if not known or n >= 2:
                    o_split(n - 2, par)

            attend(0, 0)
            attend(1, 1)
            with act.Fori(1, NCHUNK // 2) as m:
                attend(m * 2, 0)
                attend(m * 2 + 1, 1)
            attend(NCHUNK, 0)
            attend(NCHUNK + 1, 1)
            act.wait_ge(down_added, DOWN_BANKS * (DOWN_BEFORE_NORM[3] - 2))
            first_steps(3, range(4))
            last_steps(3)
            ffn(1)

        @block.vector
        def _(dve):
            def add_piece(n, q, half, copy=False):
                m, o = q // 2, q % 2
                dve.wait_ge(down_full, n * DOWN_BANKS + (q + 1))
                a = acc[:, 4 * half + m, o * HALF:(o + 1) * HALF]
                if copy:
                    nc.vector.tensor_copy(a, bank[4 + q % 2][:, :]).then_inc(down_added, 1)
                else:
                    nc.vector.tensor_tensor(a, bank[4 + q % 2][:, :], a, ALU.add).then_inc(down_added, 1)

            def add_down(n, copy=False, half=0):
                for q in range(DOWN_BANKS):
                    add_piece(n, q, half, copy)

            def x_lo(n, m, q):
                dve.wait_ge(tr_hi, m * 2 + (2 * TT * n + q + 1))
                nc.vector.tensor_tensor(XL[:, 4 * q:4 * q + 4, ds(m * P, P)],
                                        bank[6 + q][:, :].rearrange("p (k t) -> p k t", k=4),
                                        f(XH[:, 4 * q:4 * q + 4, ds(m * P, P)]), ALU.subtract).then_inc(tr_free, 1)

            def norm_step(n, k, par, has1, has2, has3, down=None):
                pre = n < 4
                base_step = STEP_BASE[n]
                one, two = has1, has2 and pre

                def piece(i):
                    if down is not None and i < len(down[1]):
                        add_piece(down[0], down[1][i], 1)

                if one or two:
                    c = slice(0 if one else 1, 2 if two else 1)
                    dve.wait_ge(sq_done, k + (SQ_BASE[n] + 1))
                    nc.vector.tensor_scalar(rms[:, c], ssq[:, c], 1.0 / D, EPS, ALU.mult, ALU.add).then_inc(ms_done, 1)
                    piece(0)
                    dve.wait_ge(root_done, k + (base_step + 1))
                    nc.vector.reciprocal(rstd[:, c], root[:, c]).then_inc(rstd_done, 1)
                    dve.wait_ge(rstd_done, k + (base_step + 1))
                if one:
                    if isinstance(k, int) and k == 0:
                        dve.wait_ge(g_loaded, 16 * n)
                    a = acc[:, ds(k, 1), :].rearrange("p a n -> p (a n)")
                    nc.vector.scalar_tensor_tensor(out=a, in0=a, scalar=rstd[:, 0:1], in1=gpost[:, :],
                                                   op0=ALU.mult, op1=ALU.mult).then_inc(scaled, 1)
                    piece(1)
                    dve.wait_ge(h_loaded[par], H_LOADS[n] + (k - par) * 8 + 16)
                    if n > 1 or not isinstance(k, int) or k > 1:
                        dve.wait_ge(h_stored[par], (k - par) * 8 + 16 * (TT // 2) * (n - 1))
                    dve.wait_ge(scaled, k + (TT * (n - 1) + 1))
                    nc.vector.tensor_tensor(hout[:, par, :], hin[:, par, :], a, ALU.add).then_inc(h_new, 1)
                    piece(2)
                if two:
                    nc.vector.tensor_scalar(acc[:, ds(k - 1, 1), :].rearrange("p a n -> p (a n)"), hout[:, 1 - par, :],
                                            rstd[:, 1:2], None, ALU.mult).then_inc(rt_ready, 1)
                piece(3)
                if has3 and pre:
                    for q in range(2):
                        x_lo(n, k - 2, q)
                        piece(4 + q)

            def first_step(n, k, down=None):
                norm_step(n, k, k % 2, True, k > 0, k > 1, down)

            def last_steps(n):
                with dve.Fori(TT // 4, TT // 2) as j:
                    norm_step(n, j * 2, 0, True, True, True)
                    norm_step(n, j * 2 + 1, 1, True, True, True)
                if n < 4:
                    norm_step(n, TT, 0, False, True, True)
                    norm_step(n, TT + 1, 1, False, False, True)

            dve.wait_ge(tr_full, 1)
            nc.vector.tensor_copy(cols[:, :], bank[6][:, 0:NCOLS]).then_inc(tr_free, 1)
            def x_normalise(b, tiles):
                c = slice(tiles[0], tiles[-1] + 1)
                dve.wait_ge(sq_done, tiles[-1] + 1)
                nc.vector.tensor_scalar(x_ms[:, c], x_ssq[:, c], 1.0 / D, EPS, ALU.mult, ALU.add).then_inc(ms_done, 1)
                dve.wait_ge(root_done, b + 1)
                nc.vector.reciprocal(x_rstd[:, c], x_root[:, c]).then_inc(rstd_done, 1)
                dve.wait_ge(rstd_done, b + 1)
                for m in tiles:
                    nc.vector.tensor_scalar(acc[:, m, :], x_tile(m), x_rstd[:, m:m + 1], None, ALU.mult).then_inc(rt_ready, 1)

            x_normalise(0, X_BATCHES[0])
            x_normalise(1, X_BATCHES[1])
            for m in range(TT // 2):
                for q in range(2):
                    x_lo(0, m, q)
            x_normalise(2, X_BATCHES[2])
            for m in range(TT // 2, TT):
                for q in range(2):
                    x_lo(0, m, q)
            dve.wait_ge(ws_loaded, 16)
            nc.vector.memset(gpost[0:CHUNK, :].rearrange("p (g j) -> p g j", g=GROUPS)[:, :, CHUNK:P], 0.0).then_inc(ws_masked, 1)
            for q in range(2):
                dve.wait_ge(tr_full, TR_WS + q + 1)
                nc.vector.tensor_copy(wsT[:, 4 * q:4 * q + 4, :], bank[6 + q][:, :].rearrange("p (g i) -> p g i", g=4)).then_inc(tr_free, 1)

            vg = raw[U][:, :].rearrange("p (m d) -> p m d", m=TT)

            def v_add_bias(i, q, first):
                idx = i * 8 + q
                if q % 4 == 0:
                    dve.wait_ge(vbias_loaded[q // 4], i * 16 + 16)
                dve.wait_ge(proj_full, idx + 1)
                if not (first and q < 2):
                    dve.wait_ge(v_act, idx - 1)
                nc.vector.tensor_tensor(sg[:, q % 2, :].rearrange("p (m d) -> p m d", m=2),
                                        bank[q % 4][:, :].rearrange("p (m d) -> p m d", m=2),
                                        vbias[:, q // 4:q // 4 + 1, :].to_broadcast([P, 2, PAIR]), ALU.add).then_inc(v_biased, 1)

            def v_stats(i, q):
                dve.wait_ge(v_act, i * 8 + q + 1)
                for m in range(2 * (q % 4), 2 * (q % 4) + 2):
                    op = nc.vector.bn_stats(stats[:, m, ds(i * 2 + q // 4, 1), :].rearrange("p a s -> p (a s)"), vg[:, m, :])
                op.then_inc(v_counted, 1)

            for q in range(8):
                v_add_bias(0, q, True)
                if q:
                    v_stats(0, q - 1)
            with dve.Fori(1, GROUPS // 2) as i:
                for q in range(8):
                    v_add_bias(i, q, False)
                    v_stats(i - int(q == 0), (q - 1) % 8)
            v_stats(GROUPS // 2 - 1, 7)
            dve.wait_ge(v_counted, V_PIECES)
            for m in range(TT):
                op = nc.vector.bn_aggr(vmean[:, m, :], stats[:, m, :, :].rearrange("p a s -> p (a s)"))
            op.then_inc(v_stat, 1)
            dve.wait_ge(v_stat, 1)
            nc.vector.tensor_scalar(vrstd[:, :], vmean[:, :, 1], EPS, None, ALU.add).then_inc(v_stat, 1)
            dve.wait_ge(v_root, 1)
            nc.vector.reciprocal(vrstd[:, :], vrstd[:, :]).then_inc(v_stat, 1)
            dve.wait_ge(v_stat, 3)

            def layer_norm(g):
                dve.wait_ge(loaded[U], g * 48 + 32)
                for m in range(TT):
                    op = nc.vector.tensor_scalar(vg[:, m, :], vg[:, m, :], vmean[:, m, 0:1], vrstd[:, m:m + 1],
                                                 ALU.subtract, ALU.mult)
                op.then_inc(ln_step, 1)
                dve.wait_ge(ln_step, g * 2 + 1)
                lg = lambda e: lngb[:, e:e + 1, :].to_broadcast([P, TT, PAIR])
                nc.vector.tensor_tensor(vg, vg, lg(0), ALU.mult).then_inc(ln_step, 1)
                dve.wait_ge(ln_step, g * 2 + 2)
                if not isinstance(g, int):
                    dve.wait_ge(mul_full, g * 4)
                nc.vector.tensor_tensor(vn[:, :, :], vg, lg(1), ALU.add).then_inc(normed_v, 1)

            def hidden_lo(st, b):
                dve.wait_ge(hid_hi, st * 2 + (b + 1))
                nc.vector.tensor_tensor(hidL[:, b, :], sg[:, b, :], f(hidH[:, b, :]), ALU.subtract).then_inc(hid_lo, 1)

            def gmlp(g, first):
                for h in range(2):
                    st = g * 2 + h
                    if not (first and h == 0):
                        add_down(g * 2 + (h - 1), half=1 - h)
                    for b in range(2):
                        dve.wait_ge(mul_full, st * 2 + (b + 1))
                        mixed = bank[2 + b][:, :].rearrange("p (m i) -> p m i", m=4)
                        nc.vector.tensor_tensor(mixed, mixed, bs[:, ds(g, 1), :].to_broadcast([P, 4, P]), ALU.add).then_inc(bias_done, 1)
                        dve.wait_ge(bias_done, st * 2 + (b + 1))
                        dve.wait_ge(act_ready, st * 2 + (b + 1))
                        nc.vector.tensor_tensor(sg[:, b, :], bank[2 + b][:, :], sg[:, b, :], ALU.mult).then_inc(prod_ready, 1)
                    for b in range(2):
                        hidden_lo(st, b)

            layer_norm(0)
            dve.wait_ge(bs_loaded, 16)
            dve.wait_ge(acc_zero, TT)
            gmlp(0, True)
            with dve.Fori(1, GMLP_CHUNKS) as g:
                layer_norm(g)
                gmlp(g, False)
            for k in range(4):
                first_step(1, k, (DOWN_FFN0 - 1, range(4 * k, 4 * k + 4)) if k < 2 else None)
            last_steps(1)

            def ffn(layer, zeroed):
                base, dbase = STAGE_FFN[layer], (DOWN_FFN0, DOWN_FFN1)[layer]
                dve.wait_ge(acc_zero, zeroed)

                def chunk(c, first, last=False):
                    for h in range(2):
                        st = c * 2 + (base + h)
                        if not (first and h == 0):
                            add_down(c * 2 + (dbase + h - 1), half=1 - h)
                        if last and h == 1:
                            for k in range(2):
                                first_step(n, k)
                        for b in range(2):
                            dve.wait_ge(mul_full, st * 2 + (b + 1))
                            dve.wait_ge(act_ready, st * 2 + (b + 1))
                            nc.vector.tensor_tensor(sg[:, b, :], bank[2 + b][:, :], sg[:, b, :], ALU.mult).then_inc(prod_ready, 1)
                        for b in range(2):
                            hidden_lo(st, b)

                n = 2 * layer + 2
                chunk(0, True)
                with dve.Fori(1, FFN_CHUNKS - 1) as c:
                    chunk(c, False)
                chunk(FFN_CHUNKS - 1, False, last=True)
                split = 5 if n < 4 else 4
                first_step(n, 2, (dbase + 2 * FFN_CHUNKS - 1, range(split)))
                first_step(n, 3, (dbase + 2 * FFN_CHUNKS - 1, range(split, DOWN_BANKS)))
                last_steps(n)

            ffn(0, 2 * TT)

            def rotate(r, e, dsts, half):
                t = slice(half * HALF, (half + 1) * HALF)
                dve.wait_ge(q_copied, r + 1)
                nc.vector.tensor_tensor(qplain[e], qplain[e], cosT[:, t], ALU.mult)
                nc.vector.tensor_tensor(qrot[e], qrot[e], sinT[:, t], ALU.mult).then_inc(rope_step, 1)
                dve.wait_ge(rope_step, r + 1)
                for rows, dst in dsts:
                    by_chunk = lambda a: a[rows, :].rearrange("p (n c) -> p n c", c=CHUNK)
                    op = nc.vector.tensor_tensor(dst, by_chunk(qplain[e]), by_chunk(qrot[e]), ALU.add)
                op.then_inc(q_done, 1)

            nc.vector.memset(vshift[0:CHUNK, 0, :], 0.0)
            for g in range(NKV):
                nc.vector.memset(kz[g][(1 - g) * HEAD:(2 - g) * HEAD, :], 0.0)
            dve.wait_ge(rope_loaded, 32)
            for h in range(2):
                rows = [slice(g * HEAD, (g + 1) * HEAD) for g in range(NKV)]
                rotate(h, h, [(rows[g], kz[g][rows[g], h * HALF:(h + 1) * HALF].rearrange("p (n c) -> p n c", c=CHUNK))
                              for g in range(NKV)], h)
            q_by_chunk = qT.rearrange("p (n t c) -> p n t c", n=NCHUNK, t=KT)
            for q in range(2 * (D // P)):
                h, tile = (q // 2) % 2, 2 * (q // 4) + q % 2
                rotate(2 + q, q % 2, [(slice(0, P), q_by_chunk[:, h * NCHUNK // 2:(h + 1) * NCHUNK // 2, tile, :])], h)

            def maxima(n, kv):
                u = n * NKV + kv
                lo = CHUNK if isinstance(n, int) and n == 0 else 0
                dve.wait_ge(s_full, u + 1)
                sc = bank[kv][:, :].rearrange("p (j m) -> p j m", j=NPAIR)[:, :, lo:P]
                nc.vector.reduce_max(a_max[:, kv, :], sc, AX_X).then_inc(s_max, 1)
                dve.wait_ge(s_max, u * 3 + 1)
                nc.vector.scalar_tensor_tensor(out=a_neg[:, kv, :], in0=a_max[:, kv, :], scalar=-SCALE, in1=neg_sink[:, kv, :],
                                               op0=ALU.mult, op1=ALU.min).then_inc(s_max, 1)
                dve.wait_ge(s_max, u * 3 + 2)
                nc.vector.tensor_tensor(a_off[:, kv, :], sink[:, kv, :], a_neg[:, kv, :], ALU.add).then_inc(s_max, 1)

            def normalise(n, kv):
                u = n * NKV + kv
                dve.wait_ge(s_exp, u + 1)
                nc.vector.tensor_tensor(a_den[:, kv, :], a_sum[:, kv, :], a_snk[:, kv, :], ALU.add).then_inc(s_norm, 1)
                dve.wait_ge(s_norm, u * 3 + 1)
                nc.vector.reciprocal(a_inv[:, kv, :], a_den[:, kv, :]).then_inc(s_norm, 1)
                dve.wait_ge(s_norm, u * 3 + 2)
                inv = a_inv[:, kv, :].unsqueeze(2).to_broadcast([P, NPAIR, P])
                nc.vector.tensor_tensor(prob[kv][:, :, :], prob[kv][:, :, :], inv, ALU.mult).then_inc(s_norm, 1)

            def o_rest(n, par):
                dve.wait_ge(o_hi, n + 1)
                nc.vector.tensor_tensor(XL[:, :, ds(n * CHUNK, CHUNK)], bank[2 + par][:, :].rearrange("p (t c) -> p t c", t=KT),
                                        f(XH[:, :, ds(n * CHUNK, CHUNK)]), ALU.subtract).then_inc(o_lo, 1)

            def attend(n, par):
                known = isinstance(n, int)
                for kv in range(NKV):
                    if not known or n < NCHUNK:
                        maxima(n, kv)
                    before = n - 1 + kv
                    if not known or 0 <= before < NCHUNK:
                        normalise(before, 1 - kv)
                    if kv == 0 and (not known or n >= 3):
                        o_rest(n - 3, 1 - par)

            dve.wait_ge(sink_loaded, 16 * 4)
            nc.vector.tensor_scalar(neg_sink[:, :, :], sink[:, :, :], -1.0, None, ALU.mult)
            for kv in range(NKV):
                nc.vector.memset(prob[kv][:, :, 0:CHUNK], 0.0)
            for n in range(4):
                attend(n, n % 2)
            with dve.Fori(2, NCHUNK // 2) as m:
                attend(m * 2, 0)
                attend(m * 2 + 1, 1)
            for n in range(NCHUNK, NCHUNK + 3):
                attend(n, n % 2)

            for i, (j, h) in enumerate(O_ORDER[:-2]):
                add_down(DOWN_O + i, copy=(j == 0), half=h)
            for k in range(4):
                first_step(3, k, (DOWN_FFN1 - 2 + k // 2, range(4 * (k % 2), 4 * (k % 2) + 4)))
            last_steps(3)
            ffn(1, 3 * TT)


DOWN_BEFORE_NORM = (0, DOWN_FFN0, DOWN_O, DOWN_FFN1, DOWN_END)
STEPS = [len(X_BATCHES), TT + 1, TT + 1, TT + 1, TT]
SQ_BASE = [0] + [TT + sum(STEPS[1:n]) for n in range(1, 5)]
STEP_BASE = [sum(STEPS[:n]) for n in range(5)]
H_LOADS = [0] + [16 * (TT // 2) * n for n in range(4)]


def rope_tables():
    pos = np.arange(S, dtype=np.float32)
    inv = (np.float32(1.0) / (np.float32(10000.0) ** (np.arange(0, HEAD, 2, dtype=np.float32) / np.float32(HEAD)))).astype(np.float32)
    ang = (inv[:, None] * pos[None, :]).astype(np.float32)
    c, s = np.cos(ang).astype(np.float32), np.sin(ang).astype(np.float32)
    return np.concatenate([c] * 4, 0), np.concatenate([-s, s, -s, s], 0)


_INS = ["x", "norm_mix_pre", "norm_mix_post", "norm_ffn_pre", "norm_ffn_post", "a_w_in", "a_b_in", "a_ln_g", "a_ln_b",
        "a_w_s", "a_b_s", "a_w_out", "kv_norm", "w_kv", "b_w_q", "b_sinks", "b_w_o", "f_w_gate_up", "f_w_down"]


def kernel(**inputs):
    import concourse.bacc as bacc
    from concourse.bass_utils import run_bass_kernel_spmd

    nc = bacc.Bacc("TRN2", target_bir_lowering=False, num_devices=1)
    cos, sin = rope_tables()
    arrays, args = {}, []
    for name in _INS + ["rope_cos", "rope_sin"]:
        a = cos if name == "rope_cos" else sin if name == "rope_sin" else np.ascontiguousarray(inputs[name])
        arrays[f"in_{name}"] = a
        args.append(nc.dram_tensor(f"in_{name}", a.shape, mybir.dt.from_np(a.dtype), kind="ExternalInput").ap())
    y = nc.dram_tensor("out_y", [1, S, D], F32, kind="ExternalOutput").ap()
    build_trunk(nc, *args, y)
    r = run_bass_kernel_spmd(nc, [arrays], core_ids=[0])
    return r.results[0]["out_y"]
```
